# Optimizing a Trainium2 kernel written in Bass

```python
import math
import jax
import jax.numpy as jnp
from jax import lax
import numpy as np

D_MODEL = 1024
BATCH = 1
SEQ = 512
DEPTH = 1
DEC_BATCH = 1
DEC_SEQ = 512
PAST_LEN = 128

F32 = jnp.float32
HEAD_DIM = 64
A_Q_HEADS = 8
A_KV_HEADS = 2
A_GROUP = A_Q_HEADS // A_KV_HEADS
Q_BLOCK = 128
GRID_W = 64
ROPE_AXIS_DIM = HEAD_DIM // 2
ROPE_THETA = 10000.0
DILATED_PAIRS = ((128, 1), (512, 4), (2048, 16))
N_DIL_GROUPS = len(DILATED_PAIRS)
B_HEADS_PER_GROUP = 4
B_HEADS = B_HEADS_PER_GROUP * N_DIL_GROUPS
N_BUCKETS = 32
MAX_DISTANCE = 1024
A_WIDTH = A_Q_HEADS * HEAD_DIM
A_KV_WIDTH = A_KV_HEADS * HEAD_DIM
B_WIDTH = B_HEADS * HEAD_DIM
B_OUT_WIDTH = B_HEADS_PER_GROUP * HEAD_DIM
IN_SPLITS = (A_WIDTH,
             A_WIDTH + A_KV_WIDTH,
             A_WIDTH + 2 * A_KV_WIDTH,
             A_WIDTH + 2 * A_KV_WIDTH + B_WIDTH,
             A_WIDTH + 2 * A_KV_WIDTH + 2 * B_WIDTH,
             A_WIDTH + 2 * A_KV_WIDTH + 3 * B_WIDTH)
IN_COLS = A_WIDTH + 2 * A_KV_WIDTH + 3 * B_WIDTH + 2 * D_MODEL
N_GROUPS = 4
EXPERTS_PER_GROUP = 4
N_EXPERTS = N_GROUPS * EXPERTS_PER_GROUP
D_EXPERT = 512
TOP_K_INNER = 2
ALPHA = (2 * DEPTH) ** 0.25
BETA = (8 * DEPTH) ** -0.25
RMS_EPS = 1e-6
LN_EPS = 1e-5
NEG_INF = -1e30

kernel_name = "hybrid_gated_gqa_dilated_hmoe_encoder"

def layer_norm(x, g, b):
    xf = x.astype(F32)
    mu = jnp.mean(xf, axis=-1, keepdims=True)
    var = jnp.mean(jnp.square(xf - mu), axis=-1, keepdims=True)
    return ((xf - mu) * lax.rsqrt(var + LN_EPS) * g.astype(F32) + b.astype(F32)).astype(x.dtype)

def rms_heads(x, g):
    xf = x.astype(F32)
    return xf * lax.rsqrt(jnp.mean(jnp.square(xf), axis=-1, keepdims=True) + RMS_EPS) * g.astype(F32)

def axial_rope_tables(s):
    rows = s // GRID_W
    row_ids = jnp.repeat(jnp.arange(rows, dtype=F32), GRID_W)
    col_ids = jnp.tile(jnp.arange(GRID_W, dtype=F32), rows)
    inv = ROPE_THETA ** (-jnp.arange(0, ROPE_AXIS_DIM, 2, dtype=F32) / ROPE_AXIS_DIM)
    ang = jnp.concatenate([row_ids[:, None] * inv, col_ids[:, None] * inv], axis=-1)
    return jnp.cos(ang), jnp.sin(ang)

def apply_axial_rope(x, cos, sin):
    half = ROPE_AXIS_DIM // 2
    c = cos[None, :, None, :]
    s = sin[None, :, None, :]

    def rot(u, cc, ss):
        u1, u2 = u[..., :half], u[..., half:]
        return jnp.concatenate([u1 * cc - u2 * ss, u2 * cc + u1 * ss], axis=-1)

    return jnp.concatenate([rot(x[..., :ROPE_AXIS_DIM], c[..., :half], s[..., :half]),
                            rot(x[..., ROPE_AXIS_DIM:], c[..., half:], s[..., half:])], axis=-1)

def t5_bucket(rel):
    half = N_BUCKETS // 2
    exact = half // 2
    n = jnp.abs(rel)
    big = exact + (jnp.log(jnp.maximum(n, 1).astype(F32) / exact)
                   / math.log(MAX_DISTANCE / exact) * (half - exact)).astype(jnp.int32)
    big = jnp.minimum(big, half - 1)
    return jnp.where(rel > 0, half, 0) + jnp.where(n < exact, n, big)

def gqa_axial_attention(q, k, v):
    b, s = q.shape[0], q.shape[1]
    nq = s // Q_BLOCK
    qb = q.reshape(b, nq, Q_BLOCK, A_KV_HEADS, A_GROUP, HEAD_DIM).transpose(1, 0, 2, 3, 4, 5)
    scale = HEAD_DIM ** -0.5

    def one_block(q_blk):
        logits = jnp.einsum('bqkgd,bskd->bkgqs', q_blk, k).astype(F32) * scale
        p = jax.nn.softmax(logits, axis=-1).astype(v.dtype)
        return jnp.einsum('bkgqs,bskd->bqkgd', p, v)

    o = lax.map(one_block, qb)
    return o.transpose(1, 0, 2, 3, 4, 5).reshape(b, s, A_WIDTH)

def dilated_window_attention(q, k, v, bias_tab, window, dilation):
    b, s, h, dh = q.shape
    r = dilation
    n = window // (2 * r)
    L = s // r
    nblk = -(-L // n)
    lp = nblk * n

    def to_sub(a):
        return a.reshape(b, L, r, h, dh).transpose(0, 2, 1, 3, 4).reshape(b * r, L, h, dh)

    qs = jnp.pad(to_sub(q), ((0, 0), (0, lp - L), (0, 0), (0, 0)))
    ks = jnp.pad(to_sub(k), ((0, 0), (n, lp - L + n), (0, 0), (0, 0)))
    vs = jnp.pad(to_sub(v), ((0, 0), (n, lp - L + n), (0, 0), (0, 0)))
    qblk = qs.reshape(b * r, nblk, n, h, dh)

    def band(a):
        ab = a.reshape(b * r, nblk + 2, n, h, dh)
        return jnp.concatenate([ab[:, :-2], ab[:, 1:-1], ab[:, 2:]], axis=2)

    kb, vb = band(ks), band(vs)
    a_idx = jnp.arange(n)
    c_idx = jnp.arange(3 * n)
    rel = c_idx[None, :] - n - a_idx[:, None]
    in_band = jnp.abs(rel) <= n
    key_pos = jnp.arange(nblk)[:, None] * n + c_idx[None, :] - n
    key_ok = (key_pos >= 0) & (key_pos < L)
    mask = in_band[None, :, :] & key_ok[:, None, :]
    bias = bias_tab[t5_bucket(rel * r)].astype(F32).transpose(2, 0, 1)

    logits = jnp.einsum('bnqhd,bnkhd->bhnqk', qblk, kb).astype(F32) * (dh ** -0.5)
    logits = jnp.where(mask[None, None], logits + bias[None, :, None], NEG_INF)
    m = jnp.max(logits, axis=-1, keepdims=True)
    p = jnp.exp(logits - m)
    den = jnp.sum(p, axis=-1)
    o = jnp.einsum('bhnqk,bnkhd->bnqhd', p.astype(vb.dtype), vb).astype(F32)
    o = o / den.transpose(0, 2, 3, 1)[..., None]
    lse = (m[..., 0] + jnp.log(den)).transpose(0, 2, 3, 1)
    o = o.reshape(b, r, lp, h, dh)[:, :, :L].transpose(0, 2, 1, 3, 4).reshape(b, s, h, dh)
    lse = lse.reshape(b, r, lp, h)[:, :, :L].transpose(0, 2, 1, 3).reshape(b, s, h)
    return o, lse

def hierarchical_moe(x, w_rg, b_rg, w_re, b_re, w_ei, w_eo):
    b, s, d = x.shape
    t = x.reshape(b * s, d)
    p_group = jax.nn.softmax((t @ w_rg).astype(F32) + b_rg.astype(F32), axis=-1)
    top_p, top_g = lax.top_k(p_group, 1)
    group_onehot = jax.nn.one_hot(top_g[:, 0], N_GROUPS, dtype=F32)
    group_gate = group_onehot * top_p
    inner_logits = jnp.einsum('td,gde->tge', t, w_re).astype(F32) + b_re.astype(F32)
    sel_logits = jnp.einsum('tge,tg->te', inner_logits, group_onehot)
    top_l, top_e = lax.top_k(sel_logits, TOP_K_INNER)
    top_w = jax.nn.softmax(top_l, axis=-1)
    inner_gate = jnp.einsum('tk,tke->te', top_w, jax.nn.one_hot(top_e, EXPERTS_PER_GROUP, dtype=F32))
    gate = (group_gate[:, :, None] * inner_gate[:, None, :]).reshape(b * s, N_EXPERTS)
    y = jnp.zeros((b * s, d), F32)
    for e in range(N_EXPERTS):
        a, u = jnp.split(t @ w_ei[e], 2, axis=-1)
        y = y + gate[:, e:e + 1] * ((jax.nn.silu(a) * u) @ w_eo[e]).astype(F32)
    return y.astype(x.dtype).reshape(b, s, d)

def encoder_layer(x, w_in, b_gate, q_gain, k_gain, rel_bias, w_branch_a, w_branch_b, w_out,
                  ln1_g, ln1_b, w_route_group, b_route_group, w_route_expert, b_route_expert,
                  w_expert_in, w_expert_out, ln2_g, ln2_b):
    b, s, _ = x.shape
    proj = x @ w_in
    qa, ka, va, qb, kb, vb, gate_pre = jnp.split(proj, list(IN_SPLITS), axis=-1)

    cos, sin = axial_rope_tables(s)
    qa = apply_axial_rope(rms_heads(qa.reshape(b, s, A_Q_HEADS, HEAD_DIM), q_gain), cos, sin).astype(x.dtype)
    ka = apply_axial_rope(rms_heads(ka.reshape(b, s, A_KV_HEADS, HEAD_DIM), k_gain), cos, sin).astype(x.dtype)
    va = va.reshape(b, s, A_KV_HEADS, HEAD_DIM)
    ya = gqa_axial_attention(qa, ka, va) @ w_branch_a

    qb = qb.reshape(b, s, N_DIL_GROUPS, B_HEADS_PER_GROUP, HEAD_DIM)
    kb = kb.reshape(b, s, N_DIL_GROUPS, B_HEADS_PER_GROUP, HEAD_DIM)
    vb = vb.reshape(b, s, N_DIL_GROUPS, B_HEADS_PER_GROUP, HEAD_DIM)
    outs, lses = [], []
    for gi, (window, dil) in enumerate(DILATED_PAIRS):
        o, l = dilated_window_attention(qb[:, :, gi], kb[:, :, gi], vb[:, :, gi],
                                        rel_bias[:, gi * B_HEADS_PER_GROUP:(gi + 1) * B_HEADS_PER_GROUP],
                                        window, dil)
        outs.append(o)
        lses.append(l)
    wts = jax.nn.softmax(jnp.stack(lses, axis=0), axis=0)
    yb = jnp.sum(wts[..., None] * jnp.stack(outs, axis=0), axis=0)
    yb = yb.reshape(b, s, B_OUT_WIDTH).astype(x.dtype) @ w_branch_b

    gates = jax.nn.sigmoid(gate_pre.astype(F32) + b_gate.astype(F32))
    g_a, g_b = jnp.split(gates, 2, axis=-1)
    merged = (g_a * ya.astype(F32) + g_b * yb.astype(F32)).astype(x.dtype)
    x = layer_norm(ALPHA * x + merged @ w_out, ln1_g, ln1_b)

    moe = hierarchical_moe(x, w_route_group, b_route_group, w_route_expert, b_route_expert,
                           w_expert_in, w_expert_out)
    return layer_norm(ALPHA * x + moe, ln2_g, ln2_b)

def setup_inputs(seed: int = 0) -> dict:
    key = jax.random.key(seed)
    ks = jax.random.split(key, 20)

    def nrm(k, shape, scale):
        return jax.random.normal(k, shape, F32) * scale

    return {
        "x_prompt": nrm(ks[0], (BATCH, SEQ, D_MODEL), 1.0),
        "x_sample": nrm(ks[1], (DEC_BATCH, DEC_SEQ, D_MODEL), 1.0),
        "w_in": nrm(ks[2], (DEPTH, D_MODEL, IN_COLS), D_MODEL ** -0.5),
        "b_gate": nrm(ks[3], (DEPTH, 2 * D_MODEL), 0.02),
        "q_gain": 1.0 + nrm(ks[4], (DEPTH, HEAD_DIM), 0.02),
        "k_gain": 1.0 + nrm(ks[5], (DEPTH, HEAD_DIM), 0.02),
        "rel_bias": nrm(ks[6], (N_BUCKETS, B_HEADS), 0.5),
        "w_branch_a": nrm(ks[7], (DEPTH, A_WIDTH, D_MODEL), A_WIDTH ** -0.5),
        "w_branch_b": nrm(ks[8], (DEPTH, B_OUT_WIDTH, D_MODEL), B_OUT_WIDTH ** -0.5),
        "w_out": nrm(ks[9], (DEPTH, D_MODEL, D_MODEL), BETA * D_MODEL ** -0.5),
        "ln1_g": 1.0 + nrm(ks[10], (DEPTH, D_MODEL), 0.02),
        "ln1_b": nrm(ks[11], (DEPTH, D_MODEL), 0.02),
        "w_route_group": nrm(ks[12], (DEPTH, D_MODEL, N_GROUPS), D_MODEL ** -0.5),
        "b_route_group": nrm(ks[13], (DEPTH, N_GROUPS), 0.01),
        "w_route_expert": nrm(ks[14], (DEPTH, N_GROUPS, D_MODEL, EXPERTS_PER_GROUP), D_MODEL ** -0.5),
        "b_route_expert": nrm(ks[15], (DEPTH, N_GROUPS, EXPERTS_PER_GROUP), 0.01),
        "w_expert_in": nrm(ks[16], (DEPTH, N_EXPERTS, D_MODEL, 2 * D_EXPERT), D_MODEL ** -0.5),
        "w_expert_out": nrm(ks[17], (DEPTH, N_EXPERTS, D_EXPERT, D_MODEL), BETA * D_EXPERT ** -0.5),
        "ln2_g": 1.0 + nrm(ks[18], (DEPTH, D_MODEL), 0.02),
        "ln2_b": nrm(ks[19], (DEPTH, D_MODEL), 0.02),
    }

def reference(x_prompt, x_sample, w_in, b_gate, q_gain, k_gain, rel_bias, w_branch_a, w_branch_b,
              w_out, ln1_g, ln1_b, w_route_group, b_route_group, w_route_expert, b_route_expert,
              w_expert_in, w_expert_out, ln2_g, ln2_b):
    def trunk(x):
        for l in range(DEPTH):
            x = encoder_layer(x, w_in[l], b_gate[l], q_gain[l], k_gain[l], rel_bias,
                              w_branch_a[l], w_branch_b[l], w_out[l], ln1_g[l], ln1_b[l],
                              w_route_group[l], b_route_group[l], w_route_expert[l], b_route_expert[l],
                              w_expert_in[l], w_expert_out[l], ln2_g[l], ln2_b[l])
        return x

    y_prompt = trunk(x_prompt)
    y_sample = trunk(x_sample)
    return (y_prompt, y_sample)


_drawn_inputs = setup_inputs


def setup_inputs(seed=0):
    import zlib

    import numpy as np

    out = dict(_drawn_inputs(seed))
    spreads = {}
    factors = {'b_gate': 23.53,
     'q_gain': 8.0,
     'k_gain': 8.0,
     'rel_bias': 3.275,
     'b_route_group': 22.687,
     'b_route_expert': 32.416,
     'ln2_g': 8.395,
     'ln2_b': 8.233}
    for name, (base, spread) in spreads.items():
        noise = np.random.default_rng([zlib.crc32(name.encode()), seed]).standard_normal(out[name].shape)
        drawn = base * np.exp(spread * noise) if base else spread * noise
        out[name] = jnp.asarray(drawn.astype(out[name].dtype))
    for name, factor in factors.items():
        out[name] = (out[name] * factor).astype(out[name].dtype)
    return out
```

```python
import concourse.bass as bass
from concourse import mybir
from contextlib import ExitStack
import math
import numpy as np

F32 = mybir.dt.float32
F32R = mybir.dt.float32r
I32 = mybir.dt.int32
ALU = mybir.AluOpType
ACT = mybir.ActivationFunctionType
X = mybir.AxisListType.X

P = 128
SEQS, SEQ, D = 2, 512, 1024
TT = SEQ // P
NT = SEQS * TT
KD = D // P
HD = 64
N_KV, GROUP = 2, 4
N_DIL, B_HEADS = 3, 4
Q_W, KV_W, B_W = 512, 128, 768
NG, EPG, DE = 4, 4, 512
NE = NG * EPG
ALPHA = 2.0 ** 0.25
RMS_EPS, LN_EPS, NEG = 1e-6, 1e-5, -1e30
SCALE = HD ** -0.5
NBUCKET = 32
TAB = 9 * 256
CW = 2048

QKV = [0, 3, 1, 4, 2, 5, 6, 7, 8, 9, 10, 11]
N_QKV, N_GATE, N_BR, N_OUT = 12, 8, 2, 4
C_GATE = N_QKV
C_A = C_GATE + N_GATE
C_B = C_A + N_BR
C_OUT = C_B + N_BR
N_CHUNK = C_OUT + N_OUT

def qkv_groups(c):
    return 2 if 3 <= c <= 8 else TT

MM_QKV = [sum(qkv_groups(c) for c in QKV[:n]) for n in range(N_QKV)]
MM_PVA = sum(qkv_groups(c) for c in QKV)
MM_PVB = MM_PVA + N_KV * GROUP
MM_GATE = MM_PVB + B_HEADS
MM_YA = MM_GATE + 2 * KD
MM_YB = MM_YA + KD
MM_OUT = MM_YB + KD
MM_N = MM_OUT + N_OUT * TT
MM_SETUP = 6 * B_HEADS
TR_X = 0
TR_Q = TR_X + 2 * TT
TR_K = TR_Q + TT
TR_A = TR_K + 2
TR_B = TR_A + N_KV * GROUP * TT
TR_X1 = TR_B + 2 * B_HEADS * TT
TR_N = TR_X1 + 2 * TT
SC_A = 0
SC_B = SC_A + N_KV * GROUP * TT
SC_R = SC_B + 2 * B_HEADS * TT
SC_N = SC_R + TT
assert MM_N % 4 == 0 and TR_N % 2 == 0 and SC_N % 2 == 0 and N_CHUNK % 2 == 0

MM_FREED, TR_FREED, SC_FREED = [], [], []
_seen = {"b_act": 0, "b_dve": 0}
for _q in QKV:
    if _q < 3:
        MM_FREED += [("q_copied", _q * TT + _t + 1) if _q < 2 else ("va_ready", _t + 1) for _t in range(TT)]
    else:
        for _g in range(qkv_groups(_q)):
            _n = ("b_act", "b_dve")[_g % 2]
            _seen[_n] += 1
            MM_FREED.append((_n, _seen[_n]))
MM_FREED += [("pv_lo", n + 1) for n in range(N_KV * GROUP + B_HEADS)] + [("gate_ready", n + 1) for n in range(2 * KD)]
MM_FREED += [("ya_used", n + 1) for n in range(KD)] + [("yb_used", n + 1) for n in range(KD)]
MM_FREED += [("residual", n + 1) for n in range(N_OUT * TT)]
TR_FREED += [("xlo", n + 1) for n in range(2 * TT)] + [("qkA_ready", n + 1) for n in range(TT + 2)]
TR_FREED += [("pt_ready", n + 1) for n in range(TR_X1 - TR_A)] + [("x1T_ready", n + 1) for n in range(2 * TT)]
SC_FREED += [("a_exp", n + 1) for n in range(SC_B)] + [("b_logit", n + 1) for n in range(SC_R - SC_B)]
SC_FREED += [("logit_ready", n + 1) for n in range(TT)]
assert (len(MM_FREED), len(TR_FREED), len(SC_FREED)) == (MM_N, TR_N, SC_N)
FREE_PER = {}
for _name, _o in MM_FREED + TR_FREED + SC_FREED:
    FREE_PER[_name] = max(_o, FREE_PER.get(_name, 0))
FREE_PER["a_exp"] = (N_KV * GROUP + B_HEADS) * TT
FREE_PER["q_copied"] = 3 * TT
FREE_BASE = {"residual": 4, "x1T_ready": 2, "logit_ready": 2}


def freed(ring, back, n, s):
    name, o = ring[n - back]
    if n < back:
        o -= FREE_PER[name]
    return name, s * FREE_PER[name] + (FREE_BASE.get(name, 0) + o)


CHUNK_END = ([MM_QKV[c] + qkv_groups(QKV[c]) for c in range(N_QKV)] + [MM_GATE + 2 * (c + 1) for c in range(N_GATE)]
             + [MM_YA + 4 * (c + 1) for c in range(2 * N_BR)] + [MM_OUT + TT * (c + 1) for c in range(N_OUT)])

SLOTS = 256
MAXTOK = SEQS * SEQ
N_SLOT = (MAXTOK // SLOTS * NE + 1) * SLOTS
NOWHERE = 4 * MAXTOK
XCH = 4
ECH = XCH + 2
RAW_E, SPLIT_E = 4, 3


class Chain:

    def __init__(self, eng, sem):
        self.eng, self.sem, self.n, self.base = eng, sem, 0, 0

    def __call__(self, ins):
        self.n += 1
        ins.then_inc(self.sem, 1)
        self.eng.wait_ge(self.sem, self.base + self.n)


DVE_CHAIN_SEQ = 2 * 3 + (N_KV * GROUP + B_HEADS) * TT + 3 + 2 * TT


def encoder_kernel(nc, x, w_in, b_gate, q_gain, k_gain, rel_bias, w_a, w_b, w_out, ln1_g, ln1_b, w_rg, b_rg,
                   w_re, b_re, w_ei, w_eo, ln2_g, ln2_b, rope_c, rope_s, bucket_sel, ident_c, before_c, ones_c,
                   expert_base_c, token_id_c, tie_c, out):
    x_v = x.rearrange("s (i c) d -> s i c d", c=TT)
    out_v = out.rearrange("s (i c) d -> s i c d", c=TT)

    toep = nc.dram_tensor("toeplitz_rows", [B_HEADS, P, TAB], F32, kind="Internal").ap()
    x1_d = nc.dram_tensor("x1_rows", [MAXTOK, D], F32, kind="Internal").ap()
    slots = nc.dram_tensor("slots", [N_SLOT, 2], I32, kind="Internal").ap()
    y_d = nc.dram_tensor("expert_rows", [2 * MAXTOK, D], F32, kind="Internal").ap()

    with ExitStack() as ctx:
        def sem(name):
            return ctx.enter_context(nc.semaphore(name))

        bank = [ctx.enter_context(nc.psum_tensor(f"bank{i}", [P, 512], F32)) for i in range(8)]
        mm_bank = lambda n: 2 + n % 4
        sc_bank = lambda n: 6 + n % 2

        arena_base = (nc.sbuf_base + 31) // 32 * 32
        at = [0]

        def place(name, cols, dt=F32):
            t = nc.alloc_sbuf_tensor_at(name, [P, cols], dt, offset=arena_base + at[0])
            at[0] += (4 * cols + 31) // 32 * 32
            assert arena_base + at[0] <= nc.sbuf_usable_end, name
            return t[:, :]

        ident = place("ident", P)
        logits = place("logits", NT * 20)
        small = place("small", 64)
        neg_max = place("neg_max", 4)
        den = place("den", 4)
        rden = place("rden", 4)
        shared_end = at[0]
        cos_q, sin_q, cos_k, sin_k = [place(n, TT * HD) for n in ("cos_q", "sin_q", "cos_k", "sin_k")]
        bgate = place("bgate", 2 * KD)
        w_route = place("w_route", KD * 20)
        b_route = place("b_route", 20)
        ss = place("ss", 3 * 16)
        stats = place("stats", TT * 12)
        mv = place("mv", TT * 2)
        rstd1 = place("rstd1", TT)
        bias_tab = place("bias_tab", B_HEADS * 9 * P)
        xT = [place(f"xT{i}", KD * SEQ, F32R) for i in range(2)]
        outA = [place(f"outA{i}", 4 * SEQ, F32R) for i in range(2)]
        outB = [place(f"outB{i}", 2 * SEQ, F32R) for i in range(2)]
        raw = [place(f"raw{i}", CW) for i in range(2)]
        whi = [place(f"whi{i}", CW, F32R) for i in range(2)]
        wlo = [place(f"wlo{i}", CW, F32R) for i in range(2)]
        kqv = place("kqv", 3 * 6 * SEQ)
        qkvA = place("qkvA", 6 * SEQ)
        prob = place("prob", 3 * 768)
        pt = place("pt", 8 * SEQ)
        xT_v = [t.rearrange("p (k n) -> p k n", k=KD) for t in xT]
        outA_v = [t.rearrange("p (k n) -> p k n", k=4) for t in outA]
        outB_v = [t.rearrange("p (k n) -> p k n", k=2) for t in outB]
        qB, kB = [kqv[:, i * 6 * SEQ:(i + 1) * 6 * SEQ].rearrange("p (f n) -> p f n", f=6) for i in range(2)]
        vB = kqv[:, 12 * SEQ:18 * SEQ].rearrange("p (t n) -> p t n", t=TT)
        x_stage = [kqv[:, 12 * SEQ + i * D:12 * SEQ + (i + 1) * D] for i in range(2)]
        sg = kqv[:, 0:16 * SEQ].rearrange("p (f n) -> p f n", f=16)
        lnp = kqv[:, 0:2 * D].rearrange("p (a n) -> p a n", a=2)
        qA = qkvA[:, 0:4 * SEQ].rearrange("p (m n) -> p m n", m=4)
        kA = qkvA[:, 4 * SEQ:5 * SEQ]
        vA = qkvA[:, 5 * SEQ:6 * SEQ].rearrange("p (t n) -> p t n", t=TT)
        gated_t = nc.alloc_sbuf_tensor_at("gated", [P, KD * SEQ], F32,
                                          offset=arena_base + at[0] - 4 * (8 * SEQ + 3 * 768 + 6 * SEQ))
        gated = gated_t[:, :].rearrange("p (f n) -> p f n", f=KD)
        x1T = [gated_t[:, i * D:(i + 1) * D].rearrange("p (k n) -> p k n", k=KD) for i in range(2)]
        q_raw = prob[:, 0:TT * 256].rearrange("p (t n) -> p t n", t=TT)
        q_tmp = prob[:, TT * 256:2 * TT * 256].rearrange("p (t n) -> p t n", t=TT)
        q_rot = pt[:, 0:TT * Q_W].rearrange("p (t m v d) -> p t m v d", t=TT, m=4, v=2)
        k_rot = pt[:, TT * Q_W:TT * (Q_W + KV_W)].rearrange("p (t n) -> p t n", t=TT)
        ptA = [pt[:, i * 4 * SEQ:(i + 1) * 4 * SEQ].rearrange("p (j n) -> p j n", j=4) for i in range(2)]
        ptB = pt[:, 0:6 * SEQ].rearrange("p (j n) -> p j n", j=6)
        xr = pt[:, 0:TT * D].rearrange("p (t n) -> p t n", t=TT)
        tabs = bias_tab.rearrange("p (h b n) -> p h b n", h=B_HEADS, b=9)
        toep_sb = [kqv[:, i * TAB:(i + 1) * TAB] for i in range(2)]
        sel_sb = pt[0:NBUCKET + 1, 0:TAB]
        rel_sb = prob[0:NBUCKET + 1, 0:12]
        rel_rep = prob[0:NBUCKET + 1, 16:16 + 12 * P].rearrange("p (h n) -> p h n", h=12)
        EMPTY = 2 * N_SLOT // P
        empty_t = nc.alloc_sbuf_tensor_at("empty_slots", [P, EMPTY], I32, offset=arena_base + at[0] - 4 * (EMPTY + 4))
        empty = empty_t[:, :].rearrange("p (n a) -> p n a", a=2)
        gains = prob[:, 1600:1600 + 2 * HD]

        at[0] = shared_end
        moe_raw = [place(f"moe_raw{i}", CW) for i in range(RAW_E)]
        moe_hi = [place(f"moe_hi{i}", CW, F32R) for i in range(SPLIT_E)]
        moe_lo = [place(f"moe_lo{i}", CW, F32R) for i in range(SPLIT_E)]
        x_rows = [place(f"x_rows{i}", 2 * D) for i in range(2)]
        xe = [[place(f"xe{n}{i}", KD * SLOTS, F32R) for n in ("h", "l")] for i in range(2)]
        silu = place("silu", 2 * SLOTS)
        h_full = place("h_full", 2 * SLOTS)
        hT = [place(f"hT{i}", 4 * SLOTS, F32R) for i in range(2)]
        y_sb = [place(f"y_sb{i}", 2 * D) for i in range(2)]
        before = place("before", P)
        ones = place("ones", P)
        expert_base = place("expert_base", NE)
        tie = place("tie", 4)
        token_id = place("token_id", 4 * NT, I32)
        wait_bearer = place("wait_bearer", 4)
        slot_ids = [place(f"slot_ids{i}", 4, I32) for i in range(2)]
        n_pass = place("n_pass", 1, I32)
        pos_i = place("pos_i", 2 * NT, I32)
        gate = place("gate", 2 * NT)
        rt = place("rt", 1600)
        ln2p = place("ln2p", 2 * D)
        fin_stats = place("fin_stats", 12 + 2 + 4)
        at[0] = shared_end
        comb = [[place(f"comb{n}{i}", D) for n in ("x", "a", "b")] for i in range(2)]

        const_in, sel_in = sem("const_in"), sem("sel_in")
        rel_ready, rep_ready, tab_act, tab_dve, tab_in = [
            sem(n) for n in ("rel_ready", "rep_ready", "tab_act", "tab_dve", "tab_in")]
        tab_out = [sem(f"tab_out{i}") for i in range(2)]
        rope_ready, zeroed, slots_zeroed = sem("rope_ready"), sem("zeroed"), sem("slots_zeroed")
        mm_done, tr_done, sc_done = sem("mm_done"), sem("tr_done"), sem("sc_done")
        x_in = [sem(f"x_in{i}") for i in range(2)]
        xhi, xlo = sem("xhi"), sem("xlo")
        raw_in = [sem(f"raw_in{i}") for i in range(2)]
        w_hi, w_split = sem("w_hi"), sem("w_split")
        q_copied, q_square, q_var, q_root, q_normed, q_turned = [
            sem(n) for n in ("q_copied", "q_square", "q_var", "q_root", "q_normed", "q_turned")]
        pool_step = sem("pool_step")
        q_mult, qkA_ready, va_ready, b_act, b_dve = [sem(n) for n in
                                                     ("q_mult", "qkA_ready", "va_ready", "b_act", "b_dve")]
        a_max, a_exp, a_scaled, pt_ready, pv_hi, pv_lo = [sem(n) for n in
                                                          ("a_max", "a_exp", "a_scaled", "pt_ready", "pv_hi", "pv_lo")]
        gate_ready, ya_used, yb_used, summed, merged_hi, merged_lo = [
            sem(n) for n in ("gate_ready", "ya_used", "yb_used", "summed", "merged_hi", "merged_lo")]
        b_logit = sem("b_logit")
        xr_in, lnp_in, residual, ln_var, ln_root, x1_ready, x1_out = [
            sem(n) for n in ("xr_in", "lnp_in", "residual", "ln_var", "ln_root", "x1_ready", "x1_out")]
        x1T_ready, logit_ready = sem("x1T_ready"), sem("logit_ready")
        dve_step, act_step = sem("dve_step"), sem("act_step")
        moe_const = sem("moe_const")
        r_exp_in, r_exp = sem("r_exp_in"), sem("r_exp")
        member, ranked, placed, counted = sem("member"), sem("ranked"), sem("placed"), sem("counted")
        scattered = sem("scattered")
        e_raw = [sem(f"e_raw{i}") for i in range(RAW_E)]
        e_hi, e_lo, e_used = sem("e_hi"), sem("e_lo"), sem("e_used")
        ids_in = [sem(f"ids_in{i}") for i in range(2)]
        bearer_ready = sem("bearer_ready")
        experts_pool, experts_dve, y_gone = sem("experts_pool"), sem("experts_dve"), sem("y_gone")
        rows_in = [sem(f"rows_in{i}") for i in range(2)]
        rows_T, xe_hi, xe_lo = sem("rows_T"), sem("xe_hi"), sem("xe_lo")
        silu_done, h_done, h_hi, h_lo = [sem(n) for n in ("silu_done", "h_done", "h_hi", "h_lo")]
        y_act, y_dve = sem("y_act"), sem("y_dve")
        y_out = [sem(f"y_out{i}") for i in range(2)]
        comb_in = [sem(f"comb_in{i}") for i in range(2)]
        f_step, f_var, f_root, f_ready, f_sum = sem("f_step"), sem("f_var"), sem("f_root"), sem("f_ready"), sem("f_sum")
        f_out = [sem(f"f_out{i}") for i in range(2)]

        by_name = {"q_copied": q_copied, "va_ready": va_ready, "b_act": b_act, "b_dve": b_dve, "pv_lo": pv_lo,
                   "gate_ready": gate_ready, "ya_used": ya_used, "yb_used": yb_used, "residual": residual, "xlo": xlo,
                   "qkA_ready": qkA_ready, "pt_ready": pt_ready, "x1T_ready": x1T_ready, "a_exp": a_exp,
                   "b_logit": b_logit, "logit_ready": logit_ready}

        block = ctx.enter_context(nc.Block())

        def chunk_parts(c):
            if c < C_A:
                n = QKV[c] if c < C_GATE else c
                v = w_in[0].rearrange("(k h p) n -> h p k n", h=2, p=HD)[:, :, :, n * 256:(n + 1) * 256]
                return [(v[h], (KD, 256)) for h in range(2)]
            if c < C_B:
                n = c - C_A
                v = w_a[0].rearrange("(h m p) n -> h p m n", h=2, p=HD)[:, :, :, n * 512:(n + 1) * 512]
                return [(v[h], (4, 512)) for h in range(2)]
            if c < C_OUT:
                n = c - C_B
                v = w_b[0].rearrange("(k h p) n -> h p k n", h=2, p=HD)[:, :, :, n * 512:(n + 1) * 512]
                return [(v[h], (2, 512)) for h in range(2)]
            n = c - C_OUT
            v = w_out[0].rearrange("(k h p) n -> h p k n", h=2, p=HD)[:, :, :, n * 256:(n + 1) * 256]
            return [(v[h], (KD, 256)) for h in range(2)]

        def chunk_shape(c):
            return chunk_parts(c)[0][1]

        def view(t, shape):
            return t[:, 0:shape[0] * shape[1]].rearrange("p (k n) -> p k n", k=shape[0])

        @block.sync
        def _(sp):
            for dst, src in ((ident, ident_c),
                             (cos_q.rearrange("p (t d) -> p t d", t=TT), rope_c),
                             (sin_q.rearrange("p (t d) -> p t d", t=TT), rope_s),
                             (gains[:, 0:HD], q_gain[0].partition_broadcast(P)),
                             (gains[:, HD:2 * HD], k_gain[0].partition_broadcast(P)),
                             (b_route[:, 0:NG], b_rg[0].partition_broadcast(P)),
                             (b_route[:, NG:20], b_re[0].rearrange("g e -> (g e)").partition_broadcast(P)),
                             (rel_sb[0:NBUCKET, :], rel_bias),
                             (sel_sb, bucket_sel)):
                sp.dma_start(dst, src).then_inc(const_in, 16)
            w_route_v = w_route.rearrange("p (k n) -> p k n", k=KD)
            with nc.allow_non_contiguous_dma(reason="a few small parameters"):
                sp.dma_start(bgate, b_gate[0].rearrange("(f p) -> p f", p=P)).then_inc(const_in, 16)
                sp.dma_start(w_route_v[:, :, 0:NG], w_rg[0].rearrange("(k p) g -> p k g", p=P)).then_inc(const_in, 16)
                for g in range(NG):
                    sp.dma_start(w_route_v[:, :, NG + EPG * g:NG + EPG * (g + 1)],
                                 w_re[0, g].rearrange("(k p) e -> p k e", p=P)).then_inc(const_in, 16)
            sp.wait_ge(zeroed, 2)
            sp.dma_start(slots.rearrange("(p n) a -> p n a", p=P), empty).then_inc(slots_zeroed, 16)
            for h in range(B_HEADS):
                sp.wait_ge(tab_act, 3 * (h + 1))
                sp.wait_ge(tab_dve, 3 * (h + 1))
                sp.dma_start(toep[h], toep_sb[h % 2]).then_inc(tab_out[h % 2], 16)
            for h in range(B_HEADS):
                sp.wait_ge(tab_out[h % 2], 16 * B_HEADS // 2)
                skew = bass.AP(toep.tensor, h * P * TAB + P - 1, [[TAB - 1, P], [256, 9], [1, P]])
                sp.dma_start(tabs[:, h], skew).then_inc(tab_in, 16)

            with sp.Fori(0, SEQS) as s:
                def load_x(t):
                    if t < 2:
                        sp.wait_ge(merged_lo, s * KD + 1)
                    else:
                        sp.wait_ge(tr_done, s * TR_N + TR_X + 2 * (t - 1))
                    sp.dma_start(x_stage[t % 2], x_v[bass.ds(s, 1), :, t].rearrange("a i d -> (a i) d")) \
                        .then_inc(x_in[t % 2], 16)

                load_x(0)
                load_x(1)
                for c in range(N_CHUNK):
                    if c == 2:
                        load_x(2)
                        load_x(3)
                    sp.wait_ge(w_split, s * N_CHUNK + c + 1)
                    for h, (src, shape) in enumerate(chunk_parts(c)):
                        sp.dma_start(view(raw[c % 2], shape)[h * HD:(h + 1) * HD], src).then_inc(raw_in[c % 2], 16)
                    if c == C_B - 1:
                        sp.wait_ge(mm_done, MM_SETUP + s * MM_N + MM_GATE)
                        sp.dma_start(xr, x_v[bass.ds(s, 1)].rearrange("a i c d -> (a i) c d")).then_inc(xr_in, 16)
                sp.wait_ge(merged_lo, s * KD + KD + 1)
                sp.dma_start(lnp[:, 0], ln1_g[0].partition_broadcast(P)).then_inc(lnp_in, 16)
                sp.dma_start(lnp[:, 1], ln1_b[0].partition_broadcast(P)).then_inc(lnp_in, 16)

            sp.wait_ge(x1_out, 16 * NT + 1)
            sp.wait_ge(logit_ready, NT + 2)
            for dst, src in ((before, before_c), (ones, ones_c), (expert_base, expert_base_c), (tie, tie_c),
                             (token_id, token_id_c), (ln2p[:, 0:D], ln2_g[0].partition_broadcast(P)),
                             (ln2p[:, D:2 * D], ln2_b[0].partition_broadcast(P))):
                sp.dma_start(dst, src).then_inc(moe_const, 16)
            sp.wait_ge(counted, 1)
            passes = sp.value_load(n_pass[0:1, 0:1], min_val=1, max_val=4)
            with sp.Fori(0, passes) as ps:
                with sp.Fori(0, NE // 2) as i:
                    for b in range(2):
                        e = i * 2 + b
                        z = ps * NE + e
                        ei = w_ei[0, bass.ds(e, 1)].rearrange("o (k p) (a m n) -> p (o k) a m n", p=P, a=2, m=XCH)
                        eo = w_eo[0, bass.ds(e, 1)].rearrange("o (c k p) n -> p (o c) k n", p=P, c=2)
                        for c in range(ECH):
                            n = b * ECH + c
                            sp.wait_ge(e_lo, (z - b) * ECH + n + 1)
                            dst = moe_raw[n % RAW_E]
                            if c < XCH:
                                v = dst.rearrange("p (k a n) -> p k a n", k=KD, a=2)
                                for a in range(2):
                                    sp.dma_start(v[:, :, a], ei[:, :, a, c]).then_inc(e_raw[n % RAW_E], 16)
                            else:
                                v = dst.rearrange("p (k n) -> p k n", k=2)
                                for k in range(2):
                                    sp.dma_start(v[:, k], eo[:, c - XCH, k]).then_inc(e_raw[n % RAW_E], 16)

            for j in range(NT):
                if j >= 2:
                    sp.wait_ge(f_out[j % 2], 16 * (j // 2))
                else:
                    sp.wait_ge(experts_dve, 1)
                    sp.wait_ge(experts_pool, 1)
                sp.dma_start(comb[j % 2][0], x1_d[j * P:(j + 1) * P, :]).then_inc(comb_in[j % 2], 16)
                for k in range(2):
                    sp.dma_start(comb[j % 2][1 + k], y_d[k * MAXTOK + j * P:k * MAXTOK + (j + 1) * P, :]) \
                        .then_inc(comb_in[j % 2], 16)
                if j >= 1:
                    sp.wait_ge(f_ready, j)
                    sp.dma_start(out_v[(j - 1) // TT, :, (j - 1) % TT], comb[(j - 1) % 2][0]) \
                        .then_inc(f_out[(j - 1) % 2], 16)
            sp.wait_ge(f_ready, NT)
            sp.dma_start(out_v[(NT - 1) // TT, :, (NT - 1) % TT], comb[(NT - 1) % 2][0]).then_inc(f_out[(NT - 1) % 2], 16)
            for b in range(2):
                sp.wait_ge(f_out[b], 16 * (NT // 2))

        @block.gpsimd
        def _(pool):
            nc.gpsimd.memset(empty[:, :, 0], 0).then_inc(zeroed, 1)
            nc.gpsimd.memset(empty[:, :, 1], NOWHERE).then_inc(zeroed, 1)
            pool.wait_ge(rope_ready, 5)
            steps = [0]
            with pool.Fori(0, SEQS) as s:
                steps[0] = 0
                pool.wait_ge(x1_out, s * 16 * TT + 1)
                for n in range(3):
                    heads, hoff = (4, 0) if n < 2 else (N_KV, 0)
                    cs, sn = (cos_q, sin_q) if n < 2 else (cos_k, sin_k)
                    pool.wait_ge(q_normed, s * 3 + n + 1)
                    for t in range(TT):
                        src = q_raw[:, t, 0:heads * HD].rearrange("p (h d) -> p h d", d=HD)
                        dst = q_rot[:, t, :, n, :] if n < 2 else k_rot[:, t, :].rearrange("p (h d) -> p h d", d=HD)
                        cos = cs[:, t * HD:(t + 1) * HD].unsqueeze(1).broadcast_to([P, heads, HD])
                        ins = nc.gpsimd.tensor_tensor(dst, src, cos, ALU.mult)
                        steps[0] += 1
                        ins.then_inc(pool_step, 1)
                        tmp = q_tmp[:, t, 0:heads * HD].rearrange("p (h a u j) -> p h a u j", h=heads, a=2, u=2)
                        s5 = q_raw[:, t, 0:heads * HD].rearrange("p (h a u j) -> p h a u j", h=heads, a=2, u=2)
                        sin = sn[:, t * HD:(t + 1) * HD].rearrange("p (a u j) -> p a u j", a=2, u=2)
                        for u in range(2):
                            ins = nc.gpsimd.tensor_tensor(
                                tmp[:, :, :, u], s5[:, :, :, 1 - u],
                                sin[:, :, u].unsqueeze(1).broadcast_to([P, heads, 2, 16]), ALU.mult)
                            steps[0] += 1
                            ins.then_inc(pool_step, 1)
                    pool.wait_ge(pool_step, s * 36 + steps[0])
                    for t in range(TT):
                        dst = q_rot[:, t, :, n, :] if n < 2 else k_rot[:, t, :].rearrange("p (h d) -> p h d", d=HD)
                        tmp = q_tmp[:, t, 0:heads * HD].rearrange("p (h d) -> p h d", d=HD)
                        ins = nc.gpsimd.tensor_tensor(dst, dst, tmp, ALU.add)
                    ins.then_inc(q_turned, 1)
            assert steps[0] == 36

            pool.wait_ge(moe_const, 16 * 7)
            pool.wait_ge(slots_zeroed, 16)
            pool.wait_ge(placed, 1)
            nc.gpsimd.memset(wait_bearer, 0).then_inc(bearer_ready, 1)
            for k in range(2):
                for j in range(NT):
                    nc.gpsimd.indirect_dma_start(
                        out=slots[:, :], out_offset=bass.IndirectOffsetOnAxis(ap=pos_i[:, k * NT + j:k * NT + j + 1], axis=0),
                        in_=token_id[:, (k * NT + j) * 2:(k * NT + j) * 2 + 2], in_offset=None).then_inc(scattered, 16)
            pool.wait_ge(scattered, 16 * 2 * NT)
            pool.wait_ge(x1_out, 16 * NT + 1)
            pool.wait_ge(counted, 1)
            passes = pool.value_load(n_pass[0:1, 0:1], min_val=1, max_val=4)

            def gather(b, z):
                for c in range(2):
                    nc.gpsimd.indirect_dma_start(
                        out=x_rows[b][:, c * D:(c + 1) * D], out_offset=None, in_=x1_d[:, :],
                        in_offset=bass.IndirectOffsetOnAxis(ap=slot_ids[b][:, 2 * c:2 * c + 1], axis=0)) \
                        .then_inc(rows_in[b], 16)

            for c in range(2):
                nc.gpsimd.dma_start(slot_ids[0][:, 2 * c:2 * c + 2], slots[c * P:(c + 1) * P, :]).then_inc(y_out[1], 16)
            pool.wait_ge(y_out[1], 32)
            gather(0, 0)
            with pool.Fori(0, passes) as ps:
                with pool.Fori(0, NE // 2) as i:
                    for b in range(2):
                        z = ps * NE + i * 2 + b
                        pair = ps * (NE // 2) + i

                        def bear(n):
                            return nc.gpsimd.tensor_tensor(wait_bearer[:, 1 + n:2 + n], wait_bearer[:, 0:1],
                                                           wait_bearer[:, 0:1], ALU.add)

                        pool.wait_ge(bearer_ready, z * 2 + 1)
                        pool.wait_ge(y_out[1 - b], pair * 32 + 32)
                        bear(0).then_inc(y_gone, 1)
                        with nc.allow_non_contiguous_dma(reason="256 pairs of numbers"):
                            nc.gpsimd.dma_start(slot_ids[1 - b].rearrange("p (c a) -> p c a", c=2),
                                                slots[bass.ds((z + 1) * SLOTS, SLOTS), :].rearrange("(c i) a -> i c a", c=2)) \
                                .then_inc(ids_in[1 - b], 16)
                        pool.wait_ge(rows_T, z * 4 + 8)
                        pool.wait_ge(ids_in[1 - b], pair * 16 + 16)
                        bear(1).then_inc(bearer_ready, 1)
                        gather(1 - b, z + 1)
                        pool.wait_ge(y_act, z * 2 + 3)
                        pool.wait_ge(y_dve, z * 2 + 3)
                        bear(2).then_inc(bearer_ready, 1)
                        for c in range(2):
                            nc.gpsimd.indirect_dma_start(
                                out=y_d[:, :], out_offset=bass.IndirectOffsetOnAxis(ap=slot_ids[b][:, 2 * c + 1:2 * c + 2], axis=0),
                                in_=y_sb[b][:, c * D:(c + 1) * D], in_offset=None, bounds_check=2 * MAXTOK - 1,
                                oob_is_err=False).then_inc(y_out[b], 16)
            pool.wait_ge(y_out[0], passes * (NE // 2) * 32)
            pool.wait_ge(y_out[1], passes * (NE // 2) * 32 + 32)
            pool.wait_ge(rows_in[0], passes * (NE // 2) * 32 + 32)
            pool.wait_ge(bearer_ready, passes * (NE * 2) + 1)
            nc.gpsimd.tensor_tensor(wait_bearer[:, 1:2], wait_bearer[:, 0:1], wait_bearer[:, 0:1], ALU.add) \
                .then_inc(experts_pool, 1)

        @block.tensor
        def _(pe):
            mm = nc.tensor.matmul

            def mm3(dst, left, right, first, last):
                mm(dst, left[0], right[1], start=first, stop=False)
                mm(dst, left[0], right[0], start=False, stop=False)
                return mm(dst, left[1], right[0], start=False, stop=last)

            pe.wait_ge(rep_ready, 1)
            n = 0
            for h in range(B_HEADS):
                for g, c0, w in [(0, 0, 512), (0, 512, 512), (0, 1024, 512), (0, 1536, 256), (1, 1792, 256), (2, 2048, 256)]:
                    if n >= 4:
                        pe.wait_ge((tab_act, tab_dve)[n % 2], (n - 4) // 2 + 1)
                    mm(bank[mm_bank(n)][:, 0:w], rel_rep[:, B_HEADS * g + h, :], sel_sb[:, c0:c0 + w],
                       start=True, stop=True).then_inc(mm_done, 1)
                    n += 1

            pe.wait_ge(tab_act, MM_SETUP // 2)
            pe.wait_ge(tab_dve, MM_SETUP // 2)

            with pe.Fori(0, SEQS) as s:
                def mm_open(n):
                    name, value = freed(MM_FREED, 4, n, s)
                    pe.wait_ge(by_name[name], value)
                    return bank[mm_bank(n)]

                def tr_open(n):
                    name, value = freed(TR_FREED, 2, n, s)
                    pe.wait_ge(by_name[name], value)
                    return bank[n % 2]

                def sc_open(n):
                    name, value = freed(SC_FREED, 2, n, s)
                    pe.wait_ge(by_name[name], value)
                    return bank[sc_bank(n)]

                for t in range(TT):
                    pe.wait_ge(x_in[t % 2], (s * 2 + t // 2) * 16 + 16)
                    for f in range(2):
                        b = tr_open(TR_X + 2 * t + f)
                        for k in range(4):
                            last = nc.tensor.transpose(b[:, k * P:(k + 1) * P],
                                                       x_stage[t % 2][:, (4 * f + k) * P:(4 * f + k + 1) * P], ident)
                        last.then_inc(tr_done, 1)
                pe.wait_ge(xlo, s * 2 * TT + 2 * TT)

                def weights(c):
                    pe.wait_ge(w_split, s * N_CHUNK + c + 3)
                    return [view(t[c % 2], chunk_shape(c)) for t in (whi, wlo)]

                def by_feature(c, n, f, ks, src):
                    b = mm_open(n)
                    w = weights(c)
                    for k in range(ks):
                        last = mm3(b[:, :], [v[:, k, f * P:(f + 1) * P] for v in w], [v[:, k, :] for v in src],
                                   k == 0, k == ks - 1)
                    last.then_inc(mm_done, 1)
                    return last

                def by_token(c, n, t, src):
                    b = mm_open(n)
                    w = weights(c)
                    for k in range(KD):
                        last = mm3(b[:, 0:256], [v[:, k, t * P:(t + 1) * P] for v in src], [v[:, k, :] for v in w],
                                   k == 0, k == KD - 1)
                    last.then_inc(mm_done, 1)
                    return last

                for c in range(N_QKV):
                    for g in range(qkv_groups(QKV[c])):
                        last = (by_feature(c, MM_QKV[c] + g, g, KD, xT_v) if qkv_groups(QKV[c]) == 2
                                else by_token(c, MM_QKV[c] + g, g, xT_v))

                pe.wait_ge(q_turned, s * 3 + 3)
                for t in range(TT):
                    b = tr_open(TR_Q + t)
                    for m in range(4):
                        last = nc.tensor.transpose(b[:, m * P:(m + 1) * P],
                                                   q_rot[:, t, m].rearrange("p v d -> p (v d)"), ident)
                    last.then_inc(tr_done, 1)
                for u in range(2):
                    b = tr_open(TR_K + u)
                    for v in range(2):
                        last = nc.tensor.transpose(b[:, v * P:(v + 1) * P], k_rot[:, 2 * u + v, :], ident)
                    last.then_inc(tr_done, 1)
                pe.wait_ge(qkA_ready, s * 6 + 6)
                pe.wait_ge(va_ready, s * TT + TT)
                NA, NB = N_KV * GROUP * TT, B_HEADS * TT
                for u in range(NA + 4):
                    if u < NA:
                        h, t = u // TT, u % TT
                        half = slice((h % 2) * HD, (h % 2) * HD + HD)
                        b = sc_open(SC_A + u)
                        mm(b[:, :], qA[half, h // 2, t * P:(t + 1) * P], kA[half, :], start=True, stop=True) \
                            .then_inc(sc_done, 1)
                    if 2 <= u < NA + 2:
                        v = u - 2
                        b = tr_open(TR_A + v)
                        pe.wait_ge(a_scaled, s * (NA + NB) + v + 1)
                        for j in range(4):
                            last = nc.tensor.transpose(b[:, j * P:(j + 1) * P],
                                                       prob[:, (v % 3) * 768 + j * P:(v % 3) * 768 + (j + 1) * P], ident)
                        last.then_inc(tr_done, 1)
                    if u >= 6 and (u - 6) % 4 == 0:
                        h = (u - 6) // 4
                        b = mm_open(MM_PVA + h)
                        pe.wait_ge(pt_ready, s * (NA + NB * 2) + TT * (h + 1))
                        for j in range(4):
                            last = mm(b[:, :], vA[:, j, :], ptA[h % 2][:, j, :], start=(j == 0), stop=(j == 3))
                        last.then_inc(mm_done, 1)

                pe.wait_ge(b_act, s * 12 + 12)
                pe.wait_ge(b_dve, s * 12 + 12)
                pe.wait_ge(tab_in, 16 * B_HEADS)
                for u in range(NB + 4):
                    if u < NB:
                        h, t = u // TT, u % TT
                        half = slice((h % 2) * HD, (h % 2) * HD + HD)
                        q = [qB[half, 2 * g + h // 2, t * P:(t + 1) * P] for g in range(N_DIL)]
                        b = sc_open(SC_B + 2 * u)
                        mm(b[:, :], q[0], kB[half, h // 2, :], start=True, stop=True).then_inc(sc_done, 1)
                        b = sc_open(SC_B + 2 * u + 1)
                        for g in (1, 2):
                            last = mm(b[:, (g - 1) * P:g * P], q[g], kB[half, 2 * g + h // 2, t * P:(t + 1) * P],
                                      start=True, stop=True)
                        last.then_inc(sc_done, 1)
                    if 2 <= u < NB + 2:
                        v = u - 2
                        pe.wait_ge(a_scaled, s * (NA + NB) + NA + v + 1)
                        for f in range(2):
                            b = tr_open(TR_B + 2 * v + f)
                            for j in range(4 if f == 0 else 2):
                                o = (v % 3) * 768 + (4 * f + j) * P
                                last = nc.tensor.transpose(b[:, j * P:(j + 1) * P], prob[:, o:o + P], ident)
                            last.then_inc(tr_done, 1)
                    if u >= 6 and (u - 6) % 4 == 0:
                        h = (u - 6) // 4
                        pair = (h // 2) * P
                        b = mm_open(MM_PVB + h)
                        pe.wait_ge(pt_ready, s * (NA + NB * 2) + NA + 2 * TT * (h + 1))
                        for j in range(4):
                            mm(b[:, :], vB[:, j, pair:pair + P], ptB[:, j, :], start=(j == 0), stop=False)
                        for g in (1, 2):
                            for t in range(TT):
                                last = mm(b[:, t * P:(t + 1) * P], vB[:, t, 256 * g + pair:256 * g + pair + P],
                                          ptB[:, 3 + g, t * P:(t + 1) * P], start=False, stop=(g == 2 and t == TT - 1))
                        last.then_inc(mm_done, 1)

                for c in range(C_GATE, C_A):
                    for f in range(2):
                        last = by_feature(c, MM_GATE + 2 * (c - C_GATE) + f, f, KD, xT_v)
                pe.wait_ge(pv_lo, s * 12 + 12)
                for c in range(C_A, C_OUT):
                    for f in range(4):
                        last = by_feature(c, MM_YA + 4 * (c - C_A) + f, f, 4 if c < C_B else 2,
                                          outA_v if c < C_B else outB_v)
                pe.wait_ge(merged_lo, s * KD + KD + 1)
                for c in range(C_OUT, N_CHUNK):
                    for t in range(TT):
                        last = by_token(c, MM_OUT + TT * (c - C_OUT) + t, t, xT_v)
                for t in range(TT):
                    pe.wait_ge(x1_ready, s * TT + t + 1)
                    for f in range(2):
                        b = tr_open(TR_X1 + 2 * t + f)
                        for k in range(4):
                            last = nc.tensor.transpose(b[:, k * P:(k + 1) * P], xr[:, t, (4 * f + k) * P:(4 * f + k + 1) * P],
                                                       ident)
                        last.then_inc(tr_done, 1)
                    b = sc_open(SC_R + t)
                    pe.wait_ge(x1T_ready, s * 2 * TT + 2 * t + 4)
                    for k in range(KD):
                        last = mm(b[:, 0:20], x1T[t % 2][:, k, :], w_route[:, k * 20:(k + 1) * 20],
                                  start=(k == 0), stop=(k == KD - 1))
                    last.then_inc(sc_done, 1)

            pe.wait_ge(member, 1)
            M16 = NT * NE
            mm(bank[2][:, 0:M16], before, rt[:, 0:M16], start=True, stop=False)
            mm(bank[2][:, 0:M16], ones, rt[:, M16:2 * M16], start=False, stop=True)
            mm(bank[3][:, 0:NE], ones, rt[:, 2 * M16:2 * M16 + NE], start=True, stop=True).then_inc(ranked, 1)
            pe.wait_ge(counted, 1)
            passes = pe.value_load(n_pass[0:1, 0:1], min_val=1, max_val=4)
            with pe.Fori(0, passes) as ps:
                with pe.Fori(0, NE // 2) as i:
                    for b in range(2):
                        z0 = ps * NE + i * 2
                        z = z0 + b
                        pe.wait_ge(rows_in[b], (ps * (NE // 2) + i) * 32 + 32)
                        for g in range(4):
                            tb = bank[g % 2]
                            pe.wait_ge(xe_lo, z * 4 + g + 1)
                            for q in range(4):
                                k, c = 2 * g + q // 2, q % 2
                                last = nc.tensor.transpose(tb[:, q * P:(q + 1) * P],
                                                           x_rows[b][:, c * D + k * P:c * D + (k + 1) * P], ident)
                            last.then_inc(rows_T, 1)
                        pe.wait_ge(xe_lo, z * 4 + 4 + 2)
                        xv = [t.rearrange("p (k n) -> p k n", k=KD) for t in xe[b]]
                        hv = [t.rearrange("p (m n) -> p m n", m=4) for t in hT]
                        for c in range(XCH):
                            n = b * ECH + c
                            ub = bank[2 + c % 2]
                            pe.wait_ge(h_done, z * XCH + c + 1)
                            pe.wait_ge(e_lo, z0 * ECH + n + RAW_E + 1)
                            w = [t[n % SPLIT_E].rearrange("p (k a n) -> p k a n", k=KD, a=2) for t in (moe_hi, moe_lo)]
                            for a in range(2):
                                for k in range(KD):
                                    last = mm3(ub[:, a * SLOTS:(a + 1) * SLOTS], [v[:, k, a] for v in w],
                                               [v[:, k] for v in xv], k == 0, k == KD - 1)
                            last.then_inc(e_used, 1)
                        for c in range(2):
                            n = b * ECH + XCH + c
                            pe.wait_ge(e_lo, z0 * ECH + n + RAW_E + 1)
                            pe.wait_ge(h_lo, z * XCH + 2 * c + 2)
                            if c == 0:
                                pe.wait_ge(y_act, z * 2 + 1)
                                pe.wait_ge(y_dve, z * 2 + 1)
                            w = [t[n % SPLIT_E].rearrange("p (k n) -> p k n", k=2) for t in (moe_hi, moe_lo)]
                            for r in range(2):
                                for d in range(2):
                                    for k in range(2):
                                        f = 2 * c + k
                                        last = mm3(bank[4 + 2 * r + d][:, :], [v[:, f, r * P:(r + 1) * P] for v in hv],
                                                   [v[:, k, d * 512:(d + 1) * 512] for v in w], f == 0, f == 3)
                            last.then_inc(e_used, 1)

        @block.scalar
        def _(act):
            A = nc.scalar.activation
            for n in range(0, MM_SETUP, 2):
                h, piece = n // 6, n % 6
                c0, w = [(0, 512), (512, 512), (1024, 512), (1536, 256), (1792, 256), (2048, 256)][piece]
                act.wait_ge(mm_done, n + 1)
                if h >= 2:
                    act.wait_ge(tab_out[h % 2], 16)
                A(toep_sb[h % 2][:, c0:c0 + w], bank[mm_bank(n)][:, 0:w], ACT.Copy) \
                    .then_inc(tab_act, 1)
            for b in range(2):
                act.wait_ge(tab_out[b], 16 * B_HEADS // 2)
            act.wait_ge(slots_zeroed, 16)

            with act.Fori(0, SEQS) as s:
                NA, NB = N_KV * GROUP * TT, B_HEADS * TT

                def mm_wait(n):
                    act.wait_ge(mm_done, MM_SETUP + s * MM_N + n + 1)
                    return bank[mm_bank(n)]

                def tr_wait(n):
                    act.wait_ge(tr_done, s * TR_N + n + 1)
                    return bank[n % 2]

                def split_hi(c):
                    shape = chunk_shape(c)
                    act.wait_ge(mm_done, MM_SETUP + s * MM_N + (CHUNK_END[c - 2] if c >= 2 else 0))
                    act.wait_ge(raw_in[c % 2], (s * (N_CHUNK // 2) + c // 2) * 32 + 32)
                    A(view(whi[c % 2], shape), view(raw[c % 2], shape), ACT.Copy).then_inc(w_hi, 1)

                split_hi(0)
                split_hi(1)
                act.wait_ge(mm_done, MM_SETUP + s * MM_N)
                for u in range(2 * TT):
                    t, f = u // 2, u % 2
                    b = tr_wait(TR_X + u)
                    A(xT_v[0][:, 4 * f:4 * f + 4, t * P:(t + 1) * P], b.rearrange("p (k n) -> p k n", k=4), ACT.Copy) \
                        .then_inc(xhi, 1)
                copied = 0
                for c in range(N_QKV):
                    n0, q = MM_QKV[c], QKV[c]
                    if q < 3:
                        if q > 0:
                            act.wait_ge(q_turned, s * 3 + q)
                        for t in range(TT):
                            b = mm_wait(n0 + t)
                            w = 256 if q < 2 else KV_W
                            A(q_raw[:, t, 0:w], b[:, 0:w], ACT.Copy).then_inc(q_copied, 1)
                            if q == 2:
                                A(vA[:, t, :], b[:, KV_W:2 * KV_W], ACT.Copy).then_inc(va_ready, 1)
                        act.wait_ge(q_copied, s * 3 * TT + (q + 1) * TT)
                        w = 256 if q < 2 else KV_W
                        A(q_tmp[:, :, 0:w], q_raw[:, :, 0:w], ACT.Square).then_inc(q_square, 1)
                    elif q <= 8:
                        b = mm_wait(n0)
                        f = 2 * (q - 3)
                        dst = qB[:, f] if f < 6 else kB[:, f - 6]
                        A(dst, b[:, :], ACT.Copy).then_inc(b_act, 1)
                    else:
                        for t in (0, 2):
                            b = mm_wait(n0 + t)
                            A(vB[:, t, (q - 9) * 256:(q - 8) * 256], b[:, 0:256], ACT.Copy) \
                                .then_inc(b_act, 1)
                    if q in (3, 4, 5):
                        m = q - 3
                        act.wait_ge(q_var, s * 3 + m + 1)
                        nh = 16 if m < 2 else 8
                        A(ss[:, m * 16:m * 16 + nh], ss[:, m * 16:m * 16 + nh], ACT.Sqrt).then_inc(q_root, 1)
                    if c + 2 < N_CHUNK:
                        split_hi(c + 2)
                for u in range(TT):
                    b = tr_wait(TR_Q + u)
                    A(qA[:, :, u * P:(u + 1) * P], b.rearrange("p (m n) -> p m n", m=4), ACT.Copy) \
                        .then_inc(qkA_ready, 1)
                for u in range(2):
                    b = tr_wait(TR_K + u)
                    A(kA[:, u * 256:(u + 1) * 256], b[:, 0:256], ACT.Copy) \
                        .then_inc(qkA_ready, 1)

                for u in range(NA + 4):
                    if u < NA:
                        act.wait_ge(a_max, s * (NA + NB) + u + 1)
                        if u >= 3:
                            act.wait_ge(tr_done, s * TR_N + TR_A + u - 2)
                        A(prob[:, (u % 3) * 768:(u % 3) * 768 + 512], bank[sc_bank(SC_A + u)][:, :], ACT.Exp,
                          bias=neg_max[:, u % 4:u % 4 + 1], scale=1.0, accum_out=den[:, u % 4:u % 4 + 1]) \
                            .then_inc(a_exp, 1)
                    if 2 <= u < NA + 2:
                        v = u - 2
                        h, t = v // TT, v % TT
                        b = tr_wait(TR_A + v)
                        if t == 0:
                            if h >= 2:
                                act.wait_ge(mm_done, MM_SETUP + s * MM_N + MM_PVA + h - 1)
                        A(ptA[h % 2][:, :, t * P:(t + 1) * P], b.rearrange("p (j n) -> p j n", j=4), ACT.Copy) \
                            .then_inc(pt_ready, 1)
                    if u >= 6 and (u - 6) % 4 == 0:
                        h = (u - 6) // 4
                        half = slice((h % 2) * HD, (h % 2) * HD + HD)
                        b = mm_wait(MM_PVA + h)
                        A(outA_v[0][half, h // 2, :], b[half, :], ACT.Copy).then_inc(pv_hi, 1)
                for u in range(NB + 4):
                    if u < NB:
                        act.wait_ge(a_max, s * (NA + NB) + NA + u + 1)
                        w = prob[:, (u % 3) * 768:(u % 3) * 768 + 768]
                        A(w, w, ACT.Exp, bias=neg_max[:, u % 4:u % 4 + 1], scale=1.0,
                          accum_out=den[:, u % 4:u % 4 + 1]).then_inc(a_exp, 1)
                    if 2 <= u < NB + 2:
                        v = u - 2
                        h, t = v // TT, v % TT
                        if t == 0:
                            act.wait_ge(mm_done, MM_SETUP + s * MM_N + MM_PVB + h)
                        for f in range(2):
                            n = TR_B + 2 * v + f
                            b = tr_wait(n)
                            js = 4 if f == 0 else 2
                            A(ptB[:, 4 * f:4 * f + js, t * P:(t + 1) * P], b[:, 0:js * P].rearrange("p (j n) -> p j n", j=js),
                              ACT.Copy).then_inc(pt_ready, 1)
                    if u >= 6 and (u - 6) % 4 == 0:
                        h = (u - 6) // 4
                        half = slice((h % 2) * HD, (h % 2) * HD + HD)
                        b = mm_wait(MM_PVB + h)
                        A(outB_v[0][half, h // 2, :], b[half, :], ACT.Copy).then_inc(pv_hi, 1)
                for c in range(C_GATE, N_CHUNK):
                    if c < C_A:
                        for f in range(2):
                            n = 2 * (c - C_GATE) + f
                            b = mm_wait(MM_GATE + n)
                            A(sg[:, n, :], b[:, :], ACT.Sigmoid, bias=bgate[:, n:n + 1]) \
                                .then_inc(gate_ready, 1)
                    if c + 2 < N_CHUNK:
                        split_hi(c + 2)
                    if C_B <= c < C_OUT:
                        for f in range(4):
                            n = 4 * (c - C_B) + f
                            act.wait_ge(summed, s * KD + n + 1)
                            A(xT_v[0][:, n, :], gated[:, n, :], ACT.Copy).then_inc(merged_hi, 1)
                act.wait_ge(ln_var, s + 1)
                A(rstd1, rstd1, ACT.Sqrt).then_inc(ln_root, 1)
                for t in range(TT):
                    act.wait_ge(x1_ready, s * TT + t + 1)
                    act.dma_start(x1_d[bass.ds(s * SEQ + t * P, P), :], xr[:, t, :]).then_inc(x1_out, 16)
                    for f in range(2):
                        n = TR_X1 + 2 * t + f
                        b = tr_wait(n)
                        if t >= 2:
                            act.wait_ge(sc_done, s * SC_N + SC_R + t - 1)
                        A(x1T[t % 2][:, 4 * f:4 * f + 4, :], b.rearrange("p (k n) -> p k n", k=4), ACT.Copy) \
                            .then_inc(x1T_ready, 1)

            act.wait_ge(r_exp_in, 1)
            A(rt[:, R_G4:R_G4 + NT * NG], rt[:, R_G4:R_G4 + NT * NG], ACT.Exp).then_inc(r_exp, 1)
            act.wait_ge(r_exp_in, 2)
            A(rt[:, R_E2:R_E2 + NT], rt[:, R_E2:R_E2 + NT], ACT.Exp).then_inc(r_exp, 1)
            act.wait_ge(counted, 1)
            passes = act.value_load(n_pass[0:1, 0:1], min_val=1, max_val=4)
            with act.Fori(0, passes) as ps:
                with act.Fori(0, NE // 2) as i:
                    z0 = ps * NE + i * 2
                    for b in range(2):
                        z = z0 + b

                        def e_split(c):
                            n = b * ECH + c
                            act.wait_ge(e_used, z0 * ECH + n + 1)
                            uses = [len([m for m in range(2 * ECH) if m % RAW_E == n % RAW_E and m <= n]), 2 * ECH // RAW_E]
                            act.wait_ge(e_raw[n % RAW_E], (ps * (NE // 2) + i) * (32 * uses[1]) + 32 * uses[0])
                            A(moe_hi[n % SPLIT_E], moe_raw[n % RAW_E], ACT.Copy).then_inc(e_hi, 1)

                        e_split(0)
                        e_split(1)
                        for g in range(4):
                            act.wait_ge(rows_T, z * 4 + g + 1 + 8)
                            A(xe[b][0][:, g * 512:(g + 1) * 512], bank[g % 2][:, :], ACT.Copy).then_inc(xe_hi, 1)
                        e_split(2)
                        for c in range(XCH):
                            act.wait_ge(e_used, SPLIT_E + z * ECH + c + 1)
                            A(silu[:, (c % 2) * SLOTS:(c % 2 + 1) * SLOTS], bank[2 + c % 2][:, 0:SLOTS], ACT.Silu) \
                                .then_inc(silu_done, 1)
                            if c + 3 < ECH:
                                e_split(c + 3)
                            act.wait_ge(h_done, z * XCH + c + 3)
                            A(hT[0][:, c * SLOTS:(c + 1) * SLOTS], h_full[:, (c % 2) * SLOTS:(c % 2 + 1) * SLOTS], ACT.Copy) \
                                .then_inc(h_hi, 1)
                        act.wait_ge(e_used, SPLIT_E + z * ECH + ECH)
                        act.wait_ge(y_gone, z + 1)
                        for d in range(2):
                            A(y_sb[b][:, d * 512:(d + 1) * 512], bank[4 + d][:, :], ACT.Copy).then_inc(y_act, 1)
            for j in range(NT):
                act.wait_ge(f_var, j + 1)
                A(fin_stats[:, 14:15], fin_stats[:, 14:15], ACT.Sqrt).then_inc(f_root, 1)

        @block.vector
        def _(dve):
            V = nc.vector
            for k, sm in enumerate([w_split] * 2 + [x1T_ready] * 2 + [logit_ready] * 2 + [residual] * 4 + [merged_lo, x1_out, y_gone]):
                V.memset(small[:, k:k + 1], 0.0).then_inc(sm, 1)
            V.memset(rel_sb[NBUCKET:NBUCKET + 1, :], 1.0).then_inc(rel_ready, 1)
            dve.wait_ge(const_in, 16 * 15)
            dve.wait_ge(rel_ready, 1)
            V.tensor_copy(rel_rep, rel_sb.unsqueeze(2).broadcast_to([NBUCKET + 1, 12, P])).then_inc(rep_ready, 1)
            gq, gk = [gains[:, i * HD:(i + 1) * HD] for i in range(2)]

            def bc(a):
                return a.unsqueeze(1).broadcast_to([P, TT, HD])

            def tab(a):
                return a.rearrange("p (t d) -> p t d", t=TT)

            def half_of(a, u):
                return a.rearrange("p (t a u j) -> p t a u j", t=TT, a=2, u=2)[:, :, :, u]

            def gain_half(g, u):
                return g.rearrange("p (a u j) -> p a u j", a=2, u=2)[:, :, u].unsqueeze(1).broadcast_to([P, TT, 2, 16])

            V.tensor_tensor(tab(cos_k), tab(cos_q), bc(gk), ALU.mult).then_inc(rope_ready, 1)
            for u in range(2):
                ins = V.tensor_tensor(half_of(sin_k, u), half_of(sin_q, u), gain_half(gk, 1 - u), ALU.mult)
            ins.then_inc(rope_ready, 1)
            V.tensor_scalar(gq, gq, SCALE, None, ALU.mult).then_inc(rope_ready, 1)
            dve.wait_ge(rope_ready, 3)
            V.tensor_tensor(tab(cos_q), tab(cos_q), bc(gq), ALU.mult).then_inc(rope_ready, 1)
            for u in range(2):
                ins = V.tensor_tensor(half_of(sin_q, u), half_of(sin_q, u), gain_half(gq, 1 - u), ALU.mult)
            ins.then_inc(rope_ready, 1)
            for n in range(1, MM_SETUP, 2):
                h, piece = n // 6, n % 6
                c0, w = [(0, 512), (512, 512), (1024, 512), (1536, 256), (1792, 256), (2048, 256)][piece]
                dve.wait_ge(mm_done, n + 1)
                if h >= 2:
                    dve.wait_ge(tab_out[h % 2], 16)
                V.tensor_copy(toep_sb[h % 2][:, c0:c0 + w], bank[mm_bank(n)][:, 0:w]) \
                    .then_inc(tab_dve, 1)
            for b in range(2):
                dve.wait_ge(tab_out[b], 16 * B_HEADS // 2)

            chain = Chain(dve, dve_step)
            with dve.Fori(0, SEQS) as s:
                NA, NB = N_KV * GROUP * TT, B_HEADS * TT
                chain.n, chain.base = 0, s * DVE_CHAIN_SEQ

                def mm_wait(n):
                    dve.wait_ge(mm_done, MM_SETUP + s * MM_N + n + 1)
                    return bank[mm_bank(n)]

                def split_lo(c):
                    shape = chunk_shape(c)
                    dve.wait_ge(w_hi, s * N_CHUNK + c + 1)
                    V.tensor_tensor(view(wlo[c % 2], shape), view(raw[c % 2], shape),
                                    view(whi[c % 2], shape).bitcast(F32), ALU.subtract).then_inc(w_split, 1)

                split_lo(0)
                split_lo(1)
                for u in range(2 * TT):
                    t, f = u // 2, u % 2
                    dve.wait_ge(xhi, s * 2 * TT + u + 1)
                    V.tensor_tensor(xT_v[1][:, 4 * f:4 * f + 4, t * P:(t + 1) * P],
                                    bank[u % 2][:, :].rearrange("p (k n) -> p k n", k=4),
                                    xT_v[0][:, 4 * f:4 * f + 4, t * P:(t + 1) * P].bitcast(F32), ALU.subtract) \
                        .then_inc(xlo, 1)
                for c in range(N_QKV):
                    n0, q = MM_QKV[c], QKV[c]
                    if q < 3:
                        w, nh = (256, 16) if q < 2 else (KV_W, 8)
                        sq = q_tmp[:, :, 0:w].rearrange("p t (h d) -> p t h d", d=HD)
                        r = ss[:, q * 16:q * 16 + nh]
                        dve.wait_ge(q_square, s * 3 + q + 1)
                        chain(V.tensor_reduce(r, sq, X, ALU.add))
                        V.tensor_scalar(r, r, 1.0 / HD, RMS_EPS, ALU.mult, ALU.add).then_inc(q_var, 1)
                    elif q <= 8:
                        b = mm_wait(n0 + 1)
                        f = 2 * (q - 3) + 1
                        dst = qB[:, f] if f < 6 else kB[:, f - 6]
                        V.tensor_copy(dst, b[:, :]).then_inc(b_dve, 1)
                    else:
                        for t in (1, 3):
                            b = mm_wait(n0 + t)
                            V.tensor_copy(vB[:, t, (q - 9) * 256:(q - 8) * 256], b[:, 0:256]) \
                                .then_inc(b_dve, 1)
                    if q in (3, 4, 5):
                        m = q - 3
                        w, nh = (256, 4) if m < 2 else (KV_W, 2)
                        r = ss[:, m * 16:m * 16 + TT * nh]
                        dve.wait_ge(q_root, s * 3 + m + 1)
                        chain(V.reciprocal(r, r))
                        v = q_raw[:, :, 0:w].rearrange("p t (h d) -> p t h d", d=HD)
                        V.tensor_tensor(v, v, r.rearrange("p (t h) -> p t h", t=TT).unsqueeze(3)
                                        .broadcast_to([P, TT, nh, HD]), ALU.mult).then_inc(q_normed, 1)
                    if c + 2 < N_CHUNK:
                        split_lo(c + 2)

                def normalise(v, width, base):
                    dve.wait_ge(a_exp, s * (NA + NB) + base + v + 1)
                    chain(V.reciprocal(rden[:, v % 4:v % 4 + 1], den[:, v % 4:v % 4 + 1]))
                    w = prob[:, (v % 3) * 768:(v % 3) * 768 + width]
                    V.tensor_scalar(w, w, rden[:, v % 4:v % 4 + 1], None, ALU.mult).then_inc(a_scaled, 1)

                for u in range(NA + 4):
                    if u < NA:
                        dve.wait_ge(sc_done, s * SC_N + SC_A + u + 1)
                        V.tensor_reduce(neg_max[:, u % 4:u % 4 + 1], bank[sc_bank(SC_A + u)][:, :], X, ALU.max, negate=True) \
                            .then_inc(a_max, 1)
                    if 1 <= u <= NA:
                        normalise(u - 1, 512, 0)
                    if u >= 6 and (u - 6) % 4 == 0:
                        h = (u - 6) // 4
                        half = slice((h % 2) * HD, (h % 2) * HD + HD)
                        dve.wait_ge(pv_hi, s * 12 + h + 1)
                        V.tensor_tensor(outA_v[1][half, h // 2, :], bank[mm_bank(MM_PVA + h)][half, :],
                                        outA_v[0][half, h // 2, :].bitcast(F32), ALU.subtract) \
                            .then_inc(pv_lo, 1)
                for u in range(NB + 4):
                    if u < NB:
                        h, t = u // TT, u % TT
                        w = prob[:, (u % 3) * 768:(u % 3) * 768 + 768]
                        dve.wait_ge(tr_done, s * TR_N + (TR_B + 2 * (u - 2) if u >= 3 else TR_B))
                        dve.wait_ge(sc_done, s * SC_N + SC_B + 2 * u + 1)
                        V.scalar_tensor_tensor(w[:, 0:512], bank[6][:, :], SCALE,
                                               tabs[:, h, 3 - t:7 - t].rearrange("p b n -> p (b n)"),
                                               ALU.mult, ALU.add).then_inc(b_logit, 1)
                        dve.wait_ge(sc_done, s * SC_N + SC_B + 2 * u + 2)
                        V.scalar_tensor_tensor(w[:, 512:768], bank[7][:, 0:256], SCALE,
                                                     tabs[:, h, 7:9].rearrange("p b n -> p (b n)"),
                                                     ALU.mult, ALU.add).then_inc(b_logit, 1)
                        dve.wait_ge(b_logit, s * 2 * NB + 2 * u + 2)
                        V.tensor_reduce(neg_max[:, u % 4:u % 4 + 1], w, X, ALU.max, negate=True).then_inc(a_max, 1)
                    if 1 <= u <= NB:
                        normalise(u - 1, 768, NA)
                    if u >= 6 and (u - 6) % 4 == 0:
                        h = (u - 6) // 4
                        half = slice((h % 2) * HD, (h % 2) * HD + HD)
                        dve.wait_ge(pv_hi, s * 12 + 8 + h + 1)
                        V.tensor_tensor(outB_v[1][half, h // 2, :], bank[mm_bank(MM_PVB + h)][half, :],
                                        outB_v[0][half, h // 2, :].bitcast(F32), ALU.subtract) \
                            .then_inc(pv_lo, 1)
                for c in range(C_GATE, N_CHUNK):
                    if C_A <= c < C_B:
                        for f in range(4):
                            n = 4 * (c - C_A) + f
                            b = mm_wait(MM_YA + n)
                            dve.wait_ge(gate_ready, s * 16 + n + 1)
                            V.tensor_tensor(gated[:, n, :], b[:, :], sg[:, n, :], ALU.mult) \
                                .then_inc(ya_used, 1)
                    if C_B <= c < C_OUT:
                        for f in range(4):
                            n = 4 * (c - C_B) + f
                            b = mm_wait(MM_YB + n)
                            dve.wait_ge(gate_ready, s * 16 + KD + n + 1)
                            V.tensor_tensor(sg[:, KD + n, :], b[:, :], sg[:, KD + n, :], ALU.mult).then_inc(yb_used, 1)
                            dve.wait_ge(yb_used, s * KD + n + 1)
                            V.tensor_tensor(gated[:, n, :], gated[:, n, :], sg[:, KD + n, :], ALU.add).then_inc(summed, 1)
                        for f in range(4):
                            n = 4 * (c - C_B) + f
                            dve.wait_ge(merged_hi, s * KD + n + 1)
                            V.tensor_tensor(xT_v[1][:, n, :], gated[:, n, :], xT_v[0][:, n, :].bitcast(F32),
                                            ALU.subtract).then_inc(merged_lo, 1)
                    if c >= C_OUT:
                        if c == C_OUT:
                            dve.wait_ge(xr_in, s * 16 + 16)
                        col = slice((c - C_OUT) * 256, (c - C_OUT + 1) * 256)
                        for t in range(TT):
                            n = MM_OUT + TT * (c - C_OUT) + t
                            b = mm_wait(n)
                            V.scalar_tensor_tensor(xr[:, t, col], xr[:, t, col], ALPHA, b[:, 0:256], ALU.mult, ALU.add) \
                                .then_inc(residual, 1)
                    if c + 2 < N_CHUNK:
                        split_lo(c + 2)
                dve.wait_ge(residual, s * TT * N_OUT + TT * N_OUT + 4)
                for t in range(TT):
                    for f in range(2):
                        ins = V.bn_stats(stats[:, t * 12 + 6 * f:t * 12 + 6 * f + 6], xr[:, t, f * 512:(f + 1) * 512])
                chain(ins)
                V.memset(small[:, 62:63], 0.0)
                for t in range(TT):
                    ins = V.bn_aggr(mv[:, 2 * t:2 * t + 2], stats[:, t * 12:t * 12 + 12])
                chain(ins)
                V.tensor_scalar(rstd1, mv.rearrange("p (t a) -> p t a", a=2)[:, :, 1], LN_EPS, None, ALU.add) \
                    .then_inc(ln_var, 1)
                dve.wait_ge(ln_root, s + 1)
                chain(V.reciprocal(rstd1, rstd1))
                dve.wait_ge(lnp_in, s * 32 + 32)
                for t in range(TT):
                    chain(V.tensor_scalar(xr[:, t, :], xr[:, t, :], mv[:, 2 * t:2 * t + 1], rstd1[:, t:t + 1],
                                          ALU.subtract, ALU.mult))
                    chain(V.tensor_tensor(xr[:, t, :], xr[:, t, :], lnp[:, 0], ALU.mult))
                    V.tensor_tensor(xr[:, t, :], xr[:, t, :], lnp[:, 1], ALU.add).then_inc(x1_ready, 1)
                for t in range(TT):
                    dve.wait_ge(sc_done, s * SC_N + SC_R + t + 1)
                    V.tensor_tensor(logits[:, bass.ds((s * TT + t) * 20, 20)], bank[sc_bank(SC_R + t)][:, 0:20],
                                    b_route, ALU.add).then_inc(logit_ready, 1)
                if chain.n != DVE_CHAIN_SEQ:
                    raise ValueError(f"DVE_CHAIN_SEQ is {chain.n}")

            dve.wait_ge(moe_const, 16 * 7)
            dve.wait_ge(logit_ready, NT + 2)
            used = 16
            for sm, k in ((e_used, SPLIT_E), (e_lo, RAW_E), (rows_T, 8), (xe_lo, 2), (h_done, 2), (y_act, 1), (y_dve, 1)):
                for _i in range(k):
                    V.memset(small[:, used:used + 1], 0.0).then_inc(sm, 1)
                    used += 1
            chain.n, chain.base = 0, SEQS * DVE_CHAIN_SEQ
            M16 = NT * NE
            lg = logits.rearrange("p (t n) -> p t n", n=20)
            area = [2 * M16 + NE]

            def r(n):
                a = rt[:, area[0]:area[0] + n]
                area[0] += n
                return a

            def bc4(a):
                return a.unsqueeze(2).broadcast_to([P, NT, 4])

            def tt(dst, a, b, op):
                chain(V.tensor_tensor(dst, a, b, op))

            def t4(a):
                return a.rearrange("p (t n) -> p t n", n=4)

            tie_b = tie.unsqueeze(1).broadcast_to([P, NT, 4])

            def first_max(dst, src, mx, tmp, tm):
                chain(V.tensor_reduce(mx, src, X, ALU.max))
                tt(t4(tmp), src, bc4(mx), ALU.is_equal)
                tt(t4(tmp), t4(tmp), tie_b, ALU.mult)
                chain(V.tensor_reduce(tm, t4(tmp), X, ALU.max))
                tt(dst, t4(tmp), bc4(tm), ALU.is_equal)

            g_hot, tmp, tm, gmax = r(NT * 4), r(NT * 4), r(NT), r(NT)
            first_max(t4(g_hot), lg[:, :, 0:4], gmax, tmp, tm)
            g4, e2 = rt[:, R_G4:R_G4 + NT * 4], rt[:, R_E2:R_E2 + NT]
            V.tensor_tensor(t4(g4), lg[:, :, 0:4], bc4(gmax), ALU.subtract).then_inc(r_exp_in, 1)
            prod, sel = r(M16), r(NT * 4)
            pv = prod.rearrange("p (t g e) -> p t g e", g=4, e=4)
            tt(pv, lg[:, :, 4:20].rearrange("p t (g e) -> p t g e", g=4),
               t4(g_hot).unsqueeze(3).broadcast_to([P, NT, 4, 4]), ALU.mult)
            chain(V.tensor_reduce(t4(sel), pv.rearrange("p t g e -> p t e g"), X, ALU.add))
            hot1, hot2, m1, m2 = r(NT * 4), r(NT * 4), r(NT), r(NT)
            first_max(t4(hot1), t4(sel), m1, tmp, tm)
            chain(V.scalar_tensor_tensor(sel, hot1, NEG, sel, ALU.mult, ALU.add))
            first_max(t4(hot2), t4(sel), m2, tmp, tm)
            V.tensor_tensor(e2, m2, m1, ALU.subtract).then_inc(r_exp_in, 1)
            one1, one2 = r(M16), r(M16)
            for one, hot in ((one1, hot1), (one2, hot2)):
                tt(one.rearrange("p (t g e) -> p t g e", g=4, e=4), t4(g_hot).unsqueeze(3).broadcast_to([P, NT, 4, 4]),
                   t4(hot).unsqueeze(2).broadcast_to([P, NT, 4, 4]), ALU.mult)
            tt(rt[:, 0:M16], one1, one2, ALU.add)
            chain(V.memset(rt[:, M16:M16 + NE], 0.0))
            for j in range(1, NT + 1):
                o = M16 + j * NE
                ins = V.tensor_tensor(rt[:, o:o + NE], rt[:, o - NE:o], rt[:, (j - 1) * NE:j * NE], ALU.add)
                if j < NT:
                    chain(ins)
            ins.then_inc(member, 1)
            dve.wait_ge(ranked, 1)
            where = r(M16)
            wv = bank[2][:, 0:M16]
            chain(V.tensor_scalar(where, wv, float(SLOTS), float((NE - 1) * SLOTS), ALU.is_ge, ALU.mult))
            for k in (2, 3):
                chain(V.tensor_scalar(prod, wv, float(SLOTS * k), float((NE - 1) * SLOTS), ALU.is_ge, ALU.mult))
                tt(where, where, prod, ALU.add)
            tt(where, where, wv, ALU.add)
            eb = expert_base.unsqueeze(1).broadcast_to([P, NT, NE])
            tt(where.rearrange("p (t e) -> p t e", e=NE), where.rearrange("p (t e) -> p t e", e=NE), eb, ALU.add)
            for k, one in enumerate((one1, one2)):
                tt(prod, one, where, ALU.mult)
                chain(V.tensor_reduce(tmp[:, k * NT:(k + 1) * NT], prod.rearrange("p (t e) -> p t e", e=NE), X, ALU.add))
            V.tensor_copy(pos_i, tmp[:, 0:2 * NT]).then_inc(placed, 1)
            over3, most = r(4), r(1)
            chain(V.tensor_reduce(most, bank[3][:, 0:NE], X, ALU.max))
            for k in range(3):
                V.tensor_scalar(over3[:, k:k + 1], most, float(SLOTS * (k + 1)), None, ALU.is_gt)
            chain(V.memset(over3[:, 3:4], 1.0))
            chain(V.tensor_reduce(most, over3, X, ALU.add))
            V.tensor_copy(n_pass[:, 0:1], most).then_inc(counted, 1)
            dve.wait_ge(r_exp, 2)
            gp = r(NT)
            chain(V.tensor_reduce(gp, t4(g4), X, ALU.add))
            chain(V.reciprocal(gp, gp))
            chain(V.tensor_scalar(m1, e2, 1.0, None, ALU.add))
            chain(V.reciprocal(m1, m1))
            tt(gate[:, 0:NT], m1, gp, ALU.mult)
            tt(gate[:, NT:2 * NT], gate[:, 0:NT], e2, ALU.mult)

            dve.wait_ge(counted, 1)
            passes = dve.value_load(n_pass[0:1, 0:1], min_val=1, max_val=4)
            with dve.Fori(0, passes) as ps:
                with dve.Fori(0, NE // 2) as i:
                    z0 = ps * NE + i * 2
                    for b in range(2):
                        z = z0 + b

                        def e_split(c):
                            n = b * ECH + c
                            dve.wait_ge(e_hi, z0 * ECH + n + 1)
                            V.tensor_tensor(moe_lo[n % SPLIT_E], moe_raw[n % RAW_E], moe_hi[n % SPLIT_E].bitcast(F32),
                                            ALU.subtract).then_inc(e_lo, 1)

                        def h_split(c):
                            dve.wait_ge(h_hi, z * XCH + c + 1)
                            V.tensor_tensor(hT[1][:, c * SLOTS:(c + 1) * SLOTS], h_full[:, (c % 2) * SLOTS:(c % 2 + 1) * SLOTS],
                                            hT[0][:, c * SLOTS:(c + 1) * SLOTS].bitcast(F32), ALU.subtract).then_inc(h_lo, 1)

                        e_split(0)
                        e_split(1)
                        for g in range(4):
                            dve.wait_ge(xe_hi, z * 4 + g + 1)
                            V.tensor_tensor(xe[b][1][:, g * 512:(g + 1) * 512], bank[g % 2][:, :],
                                            xe[b][0][:, g * 512:(g + 1) * 512].bitcast(F32), ALU.subtract).then_inc(xe_lo, 1)
                        e_split(2)
                        for c in range(XCH):
                            dve.wait_ge(silu_done, z * XCH + c + 1)
                            V.tensor_tensor(h_full[:, (c % 2) * SLOTS:(c % 2 + 1) * SLOTS],
                                            silu[:, (c % 2) * SLOTS:(c % 2 + 1) * SLOTS], bank[2 + c % 2][:, SLOTS:2 * SLOTS],
                                            ALU.mult).then_inc(h_done, 1)
                            if c + 3 < ECH:
                                e_split(c + 3)
                            h_split(c)
                        dve.wait_ge(e_used, SPLIT_E + z * ECH + ECH)
                        dve.wait_ge(y_gone, z + 1)
                        for d in range(2):
                            ins = V.tensor_copy(y_sb[b][:, D + d * 512:D + (d + 1) * 512], bank[6 + d][:, :])
                            ins.then_inc(y_dve, 1)

            V.memset(small[:, 61:62], 0.0).then_inc(experts_dve, 1)

            chain.n, chain.base = 0, 0
            chain.sem = f_step
            for j in range(NT):
                cx, ca, cb = comb[j % 2]
                dve.wait_ge(comb_in[j % 2], 48 * (j // 2 + 1))
                chain(V.tensor_scalar(cb, cb, gate[:, NT + j:NT + j + 1], None, ALU.mult))
                chain(V.scalar_tensor_tensor(ca, ca, gate[:, j:j + 1], cb, ALU.mult, ALU.add))
                V.scalar_tensor_tensor(cx, cx, ALPHA, ca, ALU.mult, ALU.add).then_inc(f_sum, 1)
                dve.wait_ge(f_sum, j + 1)
                for f in range(2):
                    ins = V.bn_stats(fin_stats[:, 6 * f:6 * f + 6], cx[:, f * 512:(f + 1) * 512])
                chain(ins)
                chain(V.bn_aggr(fin_stats[:, 12:14], fin_stats[:, 0:12]))
                V.tensor_scalar(fin_stats[:, 14:15], fin_stats[:, 13:14], LN_EPS, None, ALU.add).then_inc(f_var, 1)
                dve.wait_ge(f_root, j + 1)
                chain(V.reciprocal(fin_stats[:, 14:15], fin_stats[:, 14:15]))
                chain(V.tensor_scalar(cx, cx, fin_stats[:, 12:13], fin_stats[:, 14:15], ALU.subtract, ALU.mult))
                chain(V.tensor_tensor(cx, cx, ln2p[:, 0:D], ALU.mult))
                V.tensor_tensor(cx, cx, ln2p[:, D:2 * D], ALU.add).then_inc(f_ready, 1)


R_G4 = 2 * NT * NE + NE + 1200
R_E2 = R_G4 + NT * NG


def rope_tables():
    t = np.arange(SEQ)
    inv = 10000.0 ** (-np.arange(0, 32, 2, dtype=np.float32) / np.float32(32))
    ang = np.stack([(t // 64)[:, None] * inv[None], (t % 64)[:, None] * inv[None]], 1).astype(np.float32)
    c, s = np.cos(ang), np.sin(ang)
    cos = np.stack([c, c], 2).reshape(SEQ, HD)
    sin = np.stack([-s, s], 2).reshape(SEQ, HD)
    return [np.ascontiguousarray(a.reshape(P, TT, HD), dtype=np.float32) for a in (cos, sin)]


def bucket_rows():
    sel = np.zeros((NBUCKET + 1, 9, 256), np.float32)
    for blk in range(9):
        for u in range(255):
            d = u - (P - 1)
            if blk < 7:
                rel = 4 * d + blk - 3
                ok = abs(rel) <= 64
            elif blk == 7:
                rel, ok = 4 * d, abs(d) <= 64
            else:
                rel, ok = 4 * d, d % 4 == 0
            if not ok:
                sel[NBUCKET, blk, u] = NEG
                continue
            n = abs(rel)
            big = 8 + int(np.log(np.float32(max(n, 1)) / np.float32(8)) / np.float32(math.log(128)) * np.float32(8))
            sel[(16 if rel > 0 else 0) + (n if n < 8 else min(big, 15)), blk, u] = 1.0
    return sel.reshape(NBUCKET + 1, TAB)


def token_rows():
    tok = np.arange(P)[:, None, None] + P * np.arange(NT)[None, None, :]
    tok = np.broadcast_to(tok, (P, 2, NT))
    return np.stack([tok, tok + MAXTOK * np.arange(2)[None, :, None]], -1).reshape(P, 4 * NT).astype(np.int32)


_INS = ['w_in', 'b_gate', 'q_gain', 'k_gain', 'rel_bias', 'w_branch_a', 'w_branch_b', 'w_out', 'ln1_g', 'ln1_b',
        'w_route_group', 'b_route_group', 'w_route_expert', 'b_route_expert', 'w_expert_in', 'w_expert_out', 'ln2_g', 'ln2_b']


def kernel(**inputs):
    import numpy as _np
    import concourse.bacc as _bacc
    from concourse import mybir as _mybir
    from concourse.bass_utils import run_bass_kernel_spmd as _run

    nc = _bacc.Bacc("TRN2", target_bir_lowering=False, num_devices=1)
    arrays = {"x": _np.concatenate([_np.asarray(inputs["x_prompt"]), _np.asarray(inputs["x_sample"])], 0)}
    for n in _INS:
        arrays[n] = _np.ascontiguousarray(inputs[n])
    rc, rs = rope_tables()
    arrays.update(rope_c=rc, rope_s=rs, bucket_sel=bucket_rows(), ident_c=_np.eye(P, dtype=_np.float32),
                  before_c=_np.triu(_np.ones((P, P), _np.float32), 1), ones_c=_np.ones((P, P), _np.float32),
                  expert_base_c=_np.tile(_np.arange(NE, dtype=_np.float32) * SLOTS, (P, 1)),
                  token_id_c=token_rows(),
                  tie_c=_np.tile(_np.array([4, 3, 2, 1], _np.float32), (P, 1)))
    args = [nc.dram_tensor(f"in_{n}", a.shape, _mybir.dt.from_np(a.dtype), kind="ExternalInput").ap()
            for n, a in arrays.items()]
    args.append(nc.dram_tensor("out_dram", [SEQS, SEQ, D], _mybir.dt.float32, kind="ExternalOutput").ap())
    encoder_kernel(nc, *args)
    r = _run(nc, [{f"in_{n}": a for n, a in arrays.items()}], core_ids=[0])
    y = r.results[0]["out_dram"]
    return y[0:1], y[1:2]
```

```python
import concourse.bass as bass
from concourse import mybir
from contextlib import ExitStack
import math
import numpy as np

F32 = mybir.dt.float32
F32R = mybir.dt.float32r
I32 = mybir.dt.int32
ALU = mybir.AluOpType
ACT = mybir.ActivationFunctionType
X = mybir.AxisListType.X

P = 128
SEQS, SEQ, D = 2, 512, 1024
TT = SEQ // P
NT = SEQS * TT
KD = D // P
HD = 64
N_KV, GROUP = 2, 4
N_DIL, B_HEADS = 3, 4
Q_W, KV_W, B_W = 512, 128, 768
NG, EPG, DE = 4, 4, 512
NE = NG * EPG
ALPHA = 2.0 ** 0.25
RMS_EPS, LN_EPS, NEG = 1e-6, 1e-5, -1e30
SCALE = HD ** -0.5
NBUCKET = 32
TAB = 9 * 256
CW = 2048

QKV = [0, 3, 6, 1, 4, 7, 2, 5, 8, 9, 10, 11]
N_QKV, N_GATE, N_BR, N_OUT = 12, 8, 2, 4
C_GATE = N_QKV
C_B = C_GATE + N_GATE
C_A = C_B + N_BR
C_OUT = C_A + N_BR
N_CHUNK = C_OUT + N_OUT

def qkv_groups(c):
    return 2 if 3 <= c <= 8 else TT

MM_QKV = [sum(qkv_groups(c) for c in QKV[:n]) for n in range(N_QKV)]
MM_PVA = sum(qkv_groups(c) for c in QKV)
MM_PVB = MM_PVA + N_KV * GROUP
MM_GATE = MM_PVB + B_HEADS
MM_YB = MM_GATE + 2 * KD
MM_YA = MM_YB + KD
MM_OUT = MM_YA + KD
MM_N = MM_OUT + N_OUT * TT
TAB_PIECES = [(0, 0, 512), (0, 512, 512), (0, 1024, 512), (0, 1536, 256), (1, 1792, 256), (2, 2048, 256)]
MM_SETUP = len(TAB_PIECES)
TR_X = 0
TR_Q = TR_X + 2 * TT
TR_K = TR_Q + TT
TR_A = TR_K + 2
TR_B = TR_A + N_KV * GROUP * TT
TR_X1 = TR_B + 2 * B_HEADS * TT
TR_N = TR_X1 + 2 * TT
SC_A = 0
SC_B = SC_A + N_KV * GROUP * TT
SC_R = SC_B + 2 * B_HEADS * TT
SC_N = SC_R + TT
assert MM_N % 4 == 0 and TR_N % 2 == 0 and SC_N % 2 == 0 and N_CHUNK % 2 == 0

MM_FREED, TR_FREED, SC_FREED = [], [], []
_seen = {"b_act": 0, "b_dve": 0}
for _q in QKV:
    if _q < 3:
        MM_FREED += [("q_copied", _q * TT + _t + 1) if _q < 2 else ("va_ready", _t + 1) for _t in range(TT)]
    else:
        for _g in range(qkv_groups(_q)):
            _n = ("b_act", "b_dve")[_g % 2]
            _seen[_n] += 1
            MM_FREED.append((_n, _seen[_n]))
MM_FREED += [("pv_lo", n + 1) for n in range(N_KV * GROUP + B_HEADS)] + [("gate_ready", n + 1) for n in range(2 * KD)]
MM_FREED += [("yb_used", n + 1) for n in range(KD)] + [("ya_used", n + 1) for n in range(KD)]
MM_FREED += [("residual", n + 1) for n in range(N_OUT * TT)]
TR_FREED += [("xlo", n + 1) for n in range(2 * TT)] + [("qkA_ready", n + 1) for n in range(TT + 2)]
TR_FREED += [("pt_ready", n + 1) for n in range(TR_X1 - TR_A)] + [("x1T_ready", n + 1) for n in range(2 * TT)]
SC_FREED += [("a_exp", n + 1) for n in range(SC_B)] + [("b_logit", n + 1) for n in range(SC_R - SC_B)]
SC_FREED += [("logit_ready", n + 1) for n in range(TT)]
assert (len(MM_FREED), len(TR_FREED), len(SC_FREED)) == (MM_N, TR_N, SC_N)
FREE_PER = {}
for _name, _o in MM_FREED + TR_FREED + SC_FREED:
    FREE_PER[_name] = max(_o, FREE_PER.get(_name, 0))
FREE_PER["a_exp"] = (N_KV * GROUP + B_HEADS) * TT
FREE_PER["q_copied"] = 3 * TT
FREE_BASE = {"residual": 4, "x1T_ready": 2, "logit_ready": 2}


def freed(ring, back, n, s):
    name, o = ring[n - back]
    if n < back:
        o -= FREE_PER[name]
    return name, s * FREE_PER[name] + (FREE_BASE.get(name, 0) + o)


CHUNK_END = ([MM_QKV[c] + qkv_groups(QKV[c]) for c in range(N_QKV)] + [MM_GATE + 2 * (c + 1) for c in range(N_GATE)]
             + [MM_YB + 4 * (c + 1) for c in range(2 * N_BR)] + [MM_OUT + TT * (c + 1) for c in range(N_OUT)])

SLOTS = 256
MAXTOK = SEQS * SEQ
N_SLOT = (MAXTOK // SLOTS * NE + 3) * SLOTS
NOWHERE = 4 * MAXTOK
XCH = 4
ECH = XCH + 2
CONSTS = 16 * 13
POOL_TILES = NT - 2
RAW_E, SPLIT_E = 4, 4


class Chain:

    def __init__(self, eng, sem):
        self.eng, self.sem, self.n, self.base = eng, sem, 0, 0

    def __call__(self, ins):
        self.n += 1
        ins.then_inc(self.sem, 1)
        self.eng.wait_ge(self.sem, self.base + self.n)


DVE_CHAIN_SEQ = 2 * 3 + (N_KV * GROUP + B_HEADS) * TT + 3


def encoder_kernel(nc, x, w_in, b_gate, q_gain, k_gain, rel_bias, w_a, w_b, w_out, ln1_g, ln1_b, w_rg, b_rg,
                   w_re, b_re, w_ei, w_eo, ln2_g, ln2_b, rope_c, rope_s, bucket_sel, ident_c, before_c, ones_c,
                   expert_base_c, token_id_c, tie_c, out):
    x_v = x.rearrange("s (i c) d -> s i c d", c=TT)
    out_v = out.rearrange("s (i c) d -> s i c d", c=TT)

    tab_rows = nc.dram_tensor("bias_rows", [B_HEADS, TAB], F32, kind="Internal").ap()
    toep = nc.dram_tensor("toeplitz_rows", [B_HEADS, P, TAB], F32, kind="Internal").ap()
    x1_d = nc.dram_tensor("x1_rows", [MAXTOK, D], F32, kind="Internal").ap()
    slots = nc.dram_tensor("slots", [N_SLOT, 2], I32, kind="Internal").ap()
    y_d = nc.dram_tensor("expert_rows", [2 * MAXTOK, D], F32, kind="Internal").ap()

    with ExitStack() as ctx:
        def sem(name):
            return ctx.enter_context(nc.semaphore(name))

        bank = [ctx.enter_context(nc.psum_tensor(f"bank{i}", [P, 512], F32)) for i in range(8)]
        mm_bank = lambda n: 2 + n % 4
        sc_bank = lambda n: 6 + n % 2

        arena_base = (nc.sbuf_base + 31) // 32 * 32
        at = [0]

        def place(name, cols, dt=F32):
            t = nc.alloc_sbuf_tensor_at(name, [P, cols], dt, offset=arena_base + at[0])
            at[0] += (4 * cols + 31) // 32 * 32
            assert arena_base + at[0] <= nc.sbuf_usable_end, name
            return t[:, :]

        ident = place("ident", P)
        logits = place("logits", NT * 20)
        small = place("small", 64)
        neg_max = place("neg_max", 4)
        den = place("den", 4)
        rden = place("rden", 4)
        before = place("before", P)
        ones = place("ones", P)
        expert_base = place("expert_base", NE)
        tie = place("tie", 4)
        token_id = place("token_id", 4 * NT, I32)
        shared_end = at[0]
        cos_q, sin_q, cos_k, sin_k = [place(n, TT * HD) for n in ("cos_q", "sin_q", "cos_k", "sin_k")]
        gains = place("gains", 2 * HD)
        rel_t = place("rel_bias_rows", 12)
        bgate = place("bgate", 2 * KD)
        w_route = place("w_route", KD * 20)
        b_route = place("b_route", 20)
        ss = place("ss", 3 * 16)
        stats = place("stats", TT * N_OUT * 6)
        mv = place("mv", TT * 2)
        rstd1 = place("rstd1", TT)
        shift1 = place("shift1", TT)
        bias_tab = place("bias_tab", B_HEADS * 9 * P)
        xT = [place(f"xT{i}", KD * SEQ, F32R) for i in range(2)]
        outA = [place(f"outA{i}", 4 * SEQ, F32R) for i in range(2)]
        outB = [place(f"outB{i}", 2 * SEQ, F32R) for i in range(2)]
        raw = [place(f"raw{i}", CW) for i in range(2)]
        whi = [place(f"whi{i}", CW, F32R) for i in range(2)]
        wlo = [place(f"wlo{i}", CW, F32R) for i in range(2)]
        kqv = place("kqv", 3 * 6 * SEQ)
        qkvA = place("qkvA", 6 * SEQ)
        prob = place("prob", 3 * 768)
        pt = place("pt", 8 * SEQ)
        xT_v = [t.rearrange("p (k n) -> p k n", k=KD) for t in xT]
        outA_v = [t.rearrange("p (k n) -> p k n", k=4) for t in outA]
        outB_v = [t.rearrange("p (k n) -> p k n", k=2) for t in outB]
        qB, kB = [kqv[:, i * 6 * SEQ:(i + 1) * 6 * SEQ].rearrange("p (f n) -> p f n", f=6) for i in range(2)]
        vB = kqv[:, 12 * SEQ:18 * SEQ].rearrange("p (t n) -> p t n", t=TT)
        x_stage = [kqv[:, (2 + t) * D:(3 + t) * D] for t in range(TT)]
        sg = kqv[:, 0:16 * SEQ].rearrange("p (f n) -> p f n", f=16)
        lnp = kqv[:, 0:2 * D].rearrange("p (a n) -> p a n", a=2)
        qA = qkvA[:, 0:4 * SEQ].rearrange("p (m n) -> p m n", m=4)
        kA = qkvA[:, 4 * SEQ:5 * SEQ]
        vA = qkvA[:, 5 * SEQ:6 * SEQ].rearrange("p (t n) -> p t n", t=TT)
        gated_t = nc.alloc_sbuf_tensor_at("gated", [P, KD * SEQ], F32,
                                          offset=arena_base + at[0] - 4 * (8 * SEQ + 3 * 768 + 6 * SEQ))
        gated = gated_t[:, :].rearrange("p (f n) -> p f n", f=KD)
        x1T = [gated_t[:, i * D:(i + 1) * D].rearrange("p (k n) -> p k n", k=KD) for i in range(2)]
        q_raw = prob[:, 0:TT * 256].rearrange("p (t n) -> p t n", t=TT)
        q_tmp = prob[:, TT * 256:2 * TT * 256].rearrange("p (t n) -> p t n", t=TT)
        q_rot = pt[:, 0:TT * Q_W].rearrange("p (t m v d) -> p t m v d", t=TT, m=4, v=2)
        k_rot = pt[:, TT * Q_W:TT * (Q_W + KV_W)].rearrange("p (t n) -> p t n", t=TT)
        ptA = [pt[:, i * 4 * SEQ:(i + 1) * 4 * SEQ].rearrange("p (j n) -> p j n", j=4) for i in range(2)]
        ptB = [t[:, 0:6 * SEQ].rearrange("p (j n) -> p j n", j=6) for t in (pt, qkvA)]
        xr = pt[:, 0:TT * D].rearrange("p (t n) -> p t n", t=TT)
        tabs = bias_tab.rearrange("p (h b n) -> p h b n", h=B_HEADS, b=9)
        tab_sb = qkvA[0:B_HEADS, 0:TAB]
        sel_sb = pt[0:NBUCKET + 1, 0:TAB]
        rel_sb = rel_t[0:NBUCKET + 1, :]
        EMPTY = 2 * N_SLOT // P
        empty_t = nc.alloc_sbuf_tensor_at("empty_slots", [P, EMPTY], I32, offset=arena_base + at[0] - (4 * EMPTY + 31) // 32 * 32)
        empty = empty_t[:, :].rearrange("p (n a) -> p n a", a=2)

        at[0] = shared_end
        moe_raw = [place(f"moe_raw{i}", CW) for i in range(RAW_E)]
        moe_hi = [place(f"moe_hi{i}", CW, F32R) for i in range(SPLIT_E)]
        moe_lo = [place(f"moe_lo{i}", CW, F32R) for i in range(SPLIT_E)]
        x_rows = [place(f"x_rows{i}", 2 * D) for i in range(2)]
        rt_at = at[0] + 2 * 4 * KD * SLOTS
        xe = [[place(f"xe{n}{i}", KD * SLOTS, F32R) for n in ("h", "l")] for i in range(2)]
        silu = place("silu", 2 * SLOTS)
        h_full = place("h_full", 2 * SLOTS)
        hT = [place(f"hT{i}", 4 * SLOTS, F32R) for i in range(2)]
        y_sb = [place(f"y_sb{i}", 2 * D) for i in range(2)]
        wait_bearer = place("wait_bearer", 4)
        slot_ids = place("slot_ids", 16, I32)
        gather_ids = [slot_ids[:, 4 * i:4 * i + 4] for i in range(2)]
        scatter_ids = [slot_ids[:, 8 + 4 * i:12 + 4 * i] for i in range(2)]
        n_pass = place("n_pass", 1, I32)
        is_full = place("is_full", MAXTOK // SLOTS * NE, I32)
        pos_i = place("pos_i", 2 * NT, I32)
        gate = place("gate", 2 * NT)
        rt = nc.alloc_sbuf_tensor_at("rt", [P, 1600], F32, offset=arena_base + rt_at)[:, :]
        fin_stats = place("fin_stats", NT * 16)
        fin_mv, fin_scale, fin_shift = place("fin_mv", NT * 2), place("fin_scale", NT), place("fin_shift", NT)
        x1_tile = [place(f"x1_tile{j}", D) for j in range(NT)]
        at[0] = shared_end
        y_tile = [[place(f"y_tile{j}_{k}", D) for k in range(2)] for j in range(NT)]
        ln2p = place("ln2p", 2 * D)

        ident_in, sel_in, rope_in, const_in = sem("ident_in"), sem("sel_in"), sem("rope_in"), sem("const_in")
        rel_ready, tab_act, tab_dve, tab_out, tab_repeated, tab_in = [
            sem(n) for n in ("rel_ready", "tab_act", "tab_dve", "tab_out", "tab_repeated", "tab_in")]
        rope_ready, zeroed, slots_zeroed = sem("rope_ready"), sem("zeroed"), sem("slots_zeroed")
        mm_done, tr_done, sc_done = sem("mm_done"), sem("tr_done"), sem("sc_done")
        x_in = [sem(f"x_in{t}") for t in range(TT)]
        xhi, xlo = sem("xhi"), sem("xlo")
        raw_in = [sem(f"raw_in{i}") for i in range(2)]
        w_hi, w_split = sem("w_hi"), sem("w_split")
        q_copied, q_square, q_var, q_root, q_normed, q_turned = [
            sem(n) for n in ("q_copied", "q_square", "q_var", "q_root", "q_normed", "q_turned")]
        pool_step = sem("pool_step")
        q_mult, qkA_ready, va_ready, b_act, b_dve = [sem(n) for n in
                                                     ("q_mult", "qkA_ready", "va_ready", "b_act", "b_dve")]
        a_max, a_exp, a_scaled, pt_ready, pv_hi, pv_lo = [sem(n) for n in
                                                          ("a_max", "a_exp", "a_scaled", "pt_ready", "pv_hi", "pv_lo")]
        gate_ready, yb_used, ya_used, summed, merged_hi, merged_lo = [
            sem(n) for n in ("gate_ready", "yb_used", "ya_used", "summed", "merged_hi", "merged_lo")]
        b_logit = sem("b_logit")
        xr_in, lnp_in, residual, ln_var, ln_root, ln_scale, ln_normed, ln_gained, x1_ready, x1_out = [
            sem(n) for n in ("xr_in", "lnp_in", "residual", "ln_var", "ln_root", "ln_scale", "ln_normed", "ln_gained", "x1_ready",
                           "x1_out")]
        x1T_ready, logit_ready = sem("x1T_ready"), sem("logit_ready")
        dve_step, act_step = sem("dve_step"), sem("act_step")
        ln2_in = sem("ln2_in")
        r_exp_in, r_exp = sem("r_exp_in"), sem("r_exp")
        member, ranked, placed, counted = sem("member"), sem("ranked"), sem("placed"), sem("counted")
        scattered = sem("scattered")
        e_raw = [sem(f"e_raw{i}") for i in range(RAW_E)]
        e_hi, e_lo, e_used = sem("e_hi"), sem("e_lo"), sem("e_used")
        gather_ids_in = [sem(f"gather_ids_in{i}") for i in range(2)]
        scatter_ids_in = [sem(f"scatter_ids_in{i}") for i in range(2)]
        bearer_ready = sem("bearer_ready")
        experts_pool, experts_dve, y_gone = sem("experts_pool"), sem("experts_dve"), sem("y_gone")
        rows_in = [sem(f"rows_in{i}") for i in range(2)]
        rows_T, xe_hi, xe_lo = sem("rows_T"), sem("xe_hi"), sem("xe_lo")
        silu_done, h_done, h_turned, h_hi, h_lo = [sem(n) for n in ("silu_done", "h_done", "h_turned", "h_hi", "h_lo")]
        y_act, y_dve = sem("y_act"), sem("y_dve")
        y_out = [sem(f"y_out{i}") for i in range(2)]
        comb_in = [sem(f"comb_in{i}") for i in range(NT)]
        x1_back, f_alpha = sem("x1_back"), sem("f_alpha")
        f_step, f_var, f_root, f_scale, f_normed, f_gained, f_ready, f_last, f_out = [
            sem(n) for n in ("f_step", "f_var", "f_root", "f_scale", "f_normed", "f_gained", "f_ready", "f_last",
                           "f_out")]

        by_name = {"q_copied": q_copied, "va_ready": va_ready, "b_act": b_act, "b_dve": b_dve, "pv_lo": pv_lo,
                   "gate_ready": gate_ready, "yb_used": yb_used, "ya_used": ya_used, "residual": residual, "xlo": xlo,
                   "qkA_ready": qkA_ready, "pt_ready": pt_ready, "x1T_ready": x1T_ready, "a_exp": a_exp,
                   "b_logit": b_logit, "logit_ready": logit_ready}

        block = ctx.enter_context(nc.Block())

        def chunk_parts(c):
            if c < C_B:
                n = QKV[c] if c < C_GATE else c
                v = w_in[0].rearrange("(k h p) n -> h p k n", h=2, p=HD)[:, :, :, n * 256:(n + 1) * 256]
                return [(v[h], (KD, 256)) for h in range(2)]
            if c < C_A:
                n = c - C_B
                v = w_b[0].rearrange("(k h p) n -> h p k n", h=2, p=HD)[:, :, :, n * 512:(n + 1) * 512]
                return [(v[h], (2, 512)) for h in range(2)]
            if c < C_OUT:
                n = c - C_A
                v = w_a[0].rearrange("(h m p) n -> h p m n", h=2, p=HD)[:, :, :, n * 512:(n + 1) * 512]
                return [(v[h], (4, 512)) for h in range(2)]
            n = c - C_OUT
            v = w_out[0].rearrange("(k h p) n -> h p k n", h=2, p=HD)[:, :, :, n * 256:(n + 1) * 256]
            return [(v[h], (KD, 256)) for h in range(2)]

        def chunk_shape(c):
            return chunk_parts(c)[0][1]

        def view(t, shape):
            return t[:, 0:shape[0] * shape[1]].rearrange("p (k n) -> p k n", k=shape[0])

        @block.sync
        def _(sp):
            sp.dma_start(ident, ident_c).then_inc(ident_in, 16)
            with sp.Fori(0, SEQS) as s:
                def load_x(t):
                    sp.wait_ge(merged_lo, s * KD + 1)
                    sp.dma_start(x_stage[t], x_v[bass.ds(s, 1), :, t].rearrange("a i d -> (a i) d")).then_inc(x_in[t], 16)

                load_x(0)
                for c in range(N_CHUNK):
                    sp.wait_ge(w_split, s * N_CHUNK + c + 1)
                    for h, (src, shape) in enumerate(chunk_parts(c)):
                        sp.dma_start(view(raw[c % 2], shape)[h * HD:(h + 1) * HD], src).then_inc(raw_in[c % 2], 16)
                    if c == 0:
                        for t in range(1, TT):
                            load_x(t)
                    if c == C_A - 1:
                        sp.wait_ge(mm_done, MM_SETUP + s * MM_N + MM_GATE)
                        sp.dma_start(xr, x_v[bass.ds(s, 1)].rearrange("a i c d -> (a i) c d")).then_inc(xr_in, 16)
                sp.wait_ge(merged_lo, s * KD + KD + 1)
                sp.dma_start(lnp[:, 0], ln1_g[0].partition_broadcast(P)).then_inc(lnp_in, 16)
                sp.dma_start(lnp[:, 1], ln1_b[0].partition_broadcast(P)).then_inc(lnp_in, 16)

            sp.wait_ge(x1_out, 16 * NT + 1)
            sp.wait_ge(logit_ready, NT + 2)
            def load_pass(ps):
                with sp.Fori(0, NE // 2) as i:
                    for b in range(2):
                        e = i * 2 + b
                        z = ps * NE + e
                        ei = w_ei[0, bass.ds(e, 1)].rearrange("o (k p) (a m n) -> p (o k) a m n", p=P, a=2, m=XCH)
                        eo = w_eo[0, bass.ds(e, 1)].rearrange("o (c k p) n -> p (o c) k n", p=P, c=2)
                        for c in range(ECH):
                            n = b * ECH + c
                            sp.wait_ge(e_lo, (z - b) * ECH + n + 1)
                            dst = moe_raw[n % RAW_E]
                            if c < XCH:
                                v = dst.rearrange("p (k a n) -> p k a n", k=KD, a=2)
                                for a in range(2):
                                    sp.dma_start(v[:, :, a], ei[:, :, a, c]).then_inc(e_raw[n % RAW_E], 16)
                            else:
                                v = dst.rearrange("p (k n) -> p k n", k=2)
                                for k in range(2):
                                    sp.dma_start(v[:, k], eo[:, c - XCH, k]).then_inc(e_raw[n % RAW_E], 16)

            load_pass(0)
            sp.wait_ge(counted, 1)
            passes = sp.value_load(n_pass[0:1, 0:1], min_val=1, max_val=4)
            with sp.If(passes > 1):
                with sp.Fori(1, passes) as ps:
                    load_pass(ps)
            for c in range(SPLIT_E):
                sp.wait_ge(e_lo, passes * (NE * ECH) + c + 1)
                for a in range(2):
                    sp.dma_start(moe_raw[c % RAW_E][:, a * 16:(a + 1) * 16], ident_c[:, 0:16]).then_inc(e_raw[c % RAW_E], 16)

            sp.wait_ge(experts_dve, 1)
            sp.wait_ge(experts_pool, 1)
            for j in range(NT):
                if j == 1:
                    sp.dma_start(ln2p[:, 0:D], ln2_g[0].partition_broadcast(P)).then_inc(ln2_in, 16)
                    sp.dma_start(ln2p[:, D:2 * D], ln2_b[0].partition_broadcast(P)).then_inc(ln2_in, 16)
                for k in range(2):
                    sp.dma_start(y_tile[j][k], y_d[k * MAXTOK + j * P:k * MAXTOK + (j + 1) * P, :]).then_inc(comb_in[j], 16)
            for j in range(NT):
                if j < POOL_TILES:
                    sp.wait_ge(f_ready, j + 1)
                else:
                    sp.wait_ge(f_last, j - POOL_TILES + 1)
                sp.dma_start(out_v[j // TT, :, j % TT], x1_tile[j]).then_inc(f_out, 16)
            sp.wait_ge(f_out, 16 * NT)

        @block.gpsimd
        def _(pool):
            nc.gpsimd.memset(empty[:, :, 0], 0).then_inc(zeroed, 1)
            nc.gpsimd.memset(empty[:, :, 1], NOWHERE).then_inc(zeroed, 1)
            pool.wait_ge(zeroed, 2)
            nc.gpsimd.dma_start(slots.rearrange("(p n) a -> p n a", p=P), empty).then_inc(slots_zeroed, 16)
            pool.wait_ge(tab_act, MM_SETUP // 2)
            pool.wait_ge(tab_dve, MM_SETUP // 2)
            nc.gpsimd.dma_start(tab_rows, tab_sb).then_inc(tab_out, 16)
            pool.wait_ge(tab_out, 16)
            for h in range(B_HEADS):
                nc.gpsimd.dma_start(toep[h], tab_rows[h].partition_broadcast(P)).then_inc(tab_repeated, 16)
            pool.wait_ge(tab_repeated, 16 * B_HEADS)
            for h in range(B_HEADS):
                skew = bass.AP(toep.tensor, h * P * TAB + P - 1, [[TAB - 1, P], [256, 9], [1, P]])
                nc.gpsimd.dma_start(tabs[:, h], skew).then_inc(tab_in, 16)
            pool.wait_ge(rope_ready, 5)
            steps = [0]
            with pool.Fori(0, SEQS) as s:
                steps[0] = 0
                pool.wait_ge(x1_out, s * 16 * TT + 1)
                for n in range(3):
                    heads, hoff = (4, 0) if n < 2 else (N_KV, 0)
                    cs, sn = (cos_q, sin_q) if n < 2 else (cos_k, sin_k)
                    pool.wait_ge(q_normed, s * 3 + n + 1)
                    for t in range(TT):
                        src = q_raw[:, t, 0:heads * HD].rearrange("p (h d) -> p h d", d=HD)
                        dst = q_rot[:, t, :, n, :] if n < 2 else k_rot[:, t, :].rearrange("p (h d) -> p h d", d=HD)
                        cos = cs[:, t * HD:(t + 1) * HD].unsqueeze(1).broadcast_to([P, heads, HD])
                        ins = nc.gpsimd.tensor_tensor(dst, src, cos, ALU.mult)
                        steps[0] += 1
                        ins.then_inc(pool_step, 1)
                        tmp = q_tmp[:, t, 0:heads * HD].rearrange("p (h a u j) -> p h a u j", h=heads, a=2, u=2)
                        s5 = q_raw[:, t, 0:heads * HD].rearrange("p (h a u j) -> p h a u j", h=heads, a=2, u=2)
                        sin = sn[:, t * HD:(t + 1) * HD].rearrange("p (a u j) -> p a u j", a=2, u=2)
                        for u in range(2):
                            ins = nc.gpsimd.tensor_tensor(
                                tmp[:, :, :, u], s5[:, :, :, 1 - u],
                                sin[:, :, u].unsqueeze(1).broadcast_to([P, heads, 2, 16]), ALU.mult)
                            steps[0] += 1
                            ins.then_inc(pool_step, 1)
                    pool.wait_ge(pool_step, s * 36 + steps[0])
                    for t in range(TT):
                        dst = q_rot[:, t, :, n, :] if n < 2 else k_rot[:, t, :].rearrange("p (h d) -> p h d", d=HD)
                        tmp = q_tmp[:, t, 0:heads * HD].rearrange("p (h d) -> p h d", d=HD)
                        ins = nc.gpsimd.tensor_tensor(dst, dst, tmp, ALU.add)
                    ins.then_inc(q_turned, 1)
                for n in range(KD):
                    pool.wait_ge(ya_used, s * KD + n + 1)
                    nc.gpsimd.tensor_tensor(gated[:, n, :], gated[:, n, :], sg[:, n, :], ALU.add).then_inc(summed, 1)
                for t in range(TT):
                    if t == 0:
                        continue
                    pool.wait_ge(ln_gained, s * TT + t + 1)
                    nc.gpsimd.tensor_tensor(xr[:, t, :], xr[:, t, :], lnp[:, 1], ALU.add).then_inc(x1_ready, 1)
            assert steps[0] == 36

            pool.wait_ge(const_in, CONSTS)
            pool.wait_ge(slots_zeroed, 16)
            pool.wait_ge(placed, 1)
            nc.gpsimd.memset(wait_bearer, 0).then_inc(bearer_ready, 1)
            for k in range(2):
                for j in range(NT):
                    nc.gpsimd.indirect_dma_start(
                        out=slots[:, :], out_offset=bass.IndirectOffsetOnAxis(ap=pos_i[:, k * NT + j:k * NT + j + 1], axis=0),
                        in_=token_id[:, (k * NT + j) * 2:(k * NT + j) * 2 + 2], in_offset=None).then_inc(scattered, 16)
            pool.wait_ge(scattered, 16 * 2 * NT)
            pool.wait_ge(x1_out, 16 * NT + 1)
            pool.wait_ge(counted, 1)
            passes = pool.value_load(n_pass[0:1, 0:1], min_val=1, max_val=4)

            def load_ids(dst, z, signal):
                with nc.allow_non_contiguous_dma(reason="256 pairs of numbers"):
                    nc.gpsimd.dma_start(dst.rearrange("p (c a) -> p c a", c=2),
                                        slots[bass.ds(z * SLOTS, SLOTS), :].rearrange("(c i) a -> i c a", c=2)) \
                        .then_inc(signal, 16)

            def gather(b):
                for c in range(2):
                    nc.gpsimd.indirect_dma_start(
                        out=x_rows[b][:, c * D:(c + 1) * D], out_offset=None, in_=x1_d[:, :],
                        in_offset=bass.IndirectOffsetOnAxis(ap=gather_ids[b][:, 2 * c:2 * c + 1], axis=0)) \
                        .then_inc(rows_in[b], 16)

            for c in range(2):
                nc.gpsimd.dma_start(gather_ids[0][:, 2 * c:2 * c + 2], slots[c * P:(c + 1) * P, :]).then_inc(y_out[1], 16)
            load_ids(gather_ids[1], 1, gather_ids_in[1])
            load_ids(scatter_ids[0], 0, scatter_ids_in[0])
            pool.wait_ge(y_out[1], 32)
            gather(0)
            pool.wait_ge(gather_ids_in[1], 16)
            gather(1)
            pool.wait_ge(rows_in[0], 32)
            load_ids(gather_ids[0], 2, gather_ids_in[0])
            with pool.Fori(0, passes) as ps:
                with pool.Fori(0, NE // 2) as i:
                    for b in range(2):
                        z = ps * NE + i * 2 + b
                        pair = ps * (NE // 2) + i

                        def bear(n):
                            return nc.gpsimd.tensor_tensor(wait_bearer[:, 1 + n:2 + n], wait_bearer[:, 0:1],
                                                           wait_bearer[:, 0:1], ALU.add)

                        pool.wait_ge(bearer_ready, z * 2 + 1)
                        pool.wait_ge(rows_T, z * 4 + 12)
                        pool.wait_ge(gather_ids_in[b], pair * 16 + 16 + 16 * b)
                        bear(1).then_inc(bearer_ready, 1)
                        gather(b)
                        pool.wait_ge(y_out[1 - b], pair * 32 + 32)
                        pool.wait_ge(rows_in[1 - b], pair * 32 + 32 + 32 * b)
                        bear(0).then_inc(y_gone, 1)
                        load_ids(scatter_ids[1 - b], z + 1, scatter_ids_in[1 - b])
                        load_ids(gather_ids[1 - b], z + 3, gather_ids_in[1 - b])
                        pool.wait_ge(y_act, z * 2 + 3)
                        pool.wait_ge(y_dve, z * 2 + 3)
                        pool.wait_ge(scatter_ids_in[b], pair * 16 + 16)
                        bear(2).then_inc(bearer_ready, 1)
                        for c in range(2):
                            nc.gpsimd.indirect_dma_start(
                                out=y_d[:, :], out_offset=bass.IndirectOffsetOnAxis(ap=scatter_ids[b][:, 2 * c + 1:2 * c + 2], axis=0),
                                in_=y_sb[b][:, c * D:(c + 1) * D], in_offset=None, bounds_check=2 * MAXTOK - 1,
                                oob_is_err=False).then_inc(y_out[b], 16)
            pool.wait_ge(y_out[0], passes * (NE // 2) * 32)
            pool.wait_ge(y_out[1], passes * (NE // 2) * 32 + 32)
            pool.wait_ge(rows_in[0], passes * (NE // 2) * 32 + 32)
            pool.wait_ge(bearer_ready, passes * (NE * 2) + 1)
            pool.wait_ge(rows_in[1], passes * (NE // 2) * 32 + 32)
            pool.wait_ge(scatter_ids_in[1], passes * (NE // 2) * 16)
            for n in (*gather_ids_in, scatter_ids_in[0]):
                pool.wait_ge(n, passes * (NE // 2) * 16 + 16)
            nc.gpsimd.tensor_tensor(wait_bearer[:, 1:2], wait_bearer[:, 0:1], wait_bearer[:, 0:1], ALU.add) \
                .then_inc(experts_pool, 1)
            pool.wait_ge(ln2_in, 32)
            for j in range(POOL_TILES):
                pool.wait_ge(f_normed, j + 1)
                nc.gpsimd.tensor_tensor(x1_tile[j], x1_tile[j], ln2p[:, 0:D], ALU.mult).then_inc(f_gained, 1)
                pool.wait_ge(f_gained, j + 1)
                nc.gpsimd.tensor_tensor(x1_tile[j], x1_tile[j], ln2p[:, D:2 * D], ALU.add).then_inc(f_ready, 1)

        @block.tensor
        def _(pe):
            mm = nc.tensor.matmul

            def mm3(dst, left, right, first, last):
                mm(dst, left[0], right[1], start=first, stop=False)
                mm(dst, left[0], right[0], start=False, stop=False)
                return mm(dst, left[1], right[0], start=False, stop=last)

            pe.wait_ge(sel_in, 32)
            pe.wait_ge(rel_ready, 1)
            for n, (g, c0, w) in enumerate(TAB_PIECES):
                if n >= 4:
                    pe.wait_ge((tab_act, tab_dve)[n % 2], (n - 4) // 2 + 1)
                mm(bank[mm_bank(n)][0:B_HEADS, 0:w], rel_sb[:, B_HEADS * g:B_HEADS * (g + 1)], sel_sb[:, c0:c0 + w],
                   start=True, stop=True).then_inc(mm_done, 1)
            pe.wait_ge(tab_act, MM_SETUP // 2)
            pe.wait_ge(tab_dve, MM_SETUP // 2)
            pe.wait_ge(ident_in, 16)

            with pe.Fori(0, SEQS) as s:
                def mm_open(n):
                    name, value = freed(MM_FREED, 4, n, s)
                    pe.wait_ge(by_name[name], value)
                    return bank[mm_bank(n)]

                def tr_open(n):
                    name, value = freed(TR_FREED, 2, n, s)
                    pe.wait_ge(by_name[name], value)
                    return bank[n % 2]

                def sc_open(n):
                    name, value = freed(SC_FREED, 2, n, s)
                    pe.wait_ge(by_name[name], value)
                    return bank[sc_bank(n)]

                for t in range(TT):
                    pe.wait_ge(x_in[t], s * 16 + 16)
                    for f in range(2):
                        b = tr_open(TR_X + 2 * t + f)
                        for k in range(4):
                            last = nc.tensor.transpose(b[:, k * P:(k + 1) * P],
                                                       x_stage[t][:, (4 * f + k) * P:(4 * f + k + 1) * P], ident)
                        last.then_inc(tr_done, 1)
                pe.wait_ge(xlo, s * 2 * TT + 2 * TT)

                def weights(c):
                    pe.wait_ge(w_split, s * N_CHUNK + c + 3)
                    return [view(t[c % 2], chunk_shape(c)) for t in (whi, wlo)]

                def by_feature(c, n, f, ks, src):
                    b = mm_open(n)
                    w = weights(c)
                    for k in range(ks):
                        last = mm3(b[:, :], [v[:, k, f * P:(f + 1) * P] for v in w], [v[:, k, :] for v in src],
                                   k == 0, k == ks - 1)
                    last.then_inc(mm_done, 1)
                    return last

                def by_token(c, n, t, src):
                    b = mm_open(n)
                    w = weights(c)
                    for k in range(KD):
                        if n == MM_OUT:
                            pe.wait_ge(merged_lo, s * KD + k + 2)
                        last = mm3(b[:, 0:256], [v[:, k, t * P:(t + 1) * P] for v in src], [v[:, k, :] for v in w],
                                   k == 0, k == KD - 1)
                    last.then_inc(mm_done, 1)
                    return last

                for c in range(N_QKV):
                    for g in range(qkv_groups(QKV[c])):
                        last = (by_feature(c, MM_QKV[c] + g, g, KD, xT_v) if qkv_groups(QKV[c]) == 2
                                else by_token(c, MM_QKV[c] + g, g, xT_v))

                pe.wait_ge(q_turned, s * 3 + 3)
                for t in range(TT):
                    b = tr_open(TR_Q + t)
                    for m in range(4):
                        last = nc.tensor.transpose(b[:, m * P:(m + 1) * P],
                                                   q_rot[:, t, m].rearrange("p v d -> p (v d)"), ident)
                    last.then_inc(tr_done, 1)
                for u in range(2):
                    b = tr_open(TR_K + u)
                    for v in range(2):
                        last = nc.tensor.transpose(b[:, v * P:(v + 1) * P], k_rot[:, 2 * u + v, :], ident)
                    last.then_inc(tr_done, 1)
                pe.wait_ge(qkA_ready, s * 6 + 6)
                pe.wait_ge(va_ready, s * TT + TT)
                NA, NB = N_KV * GROUP * TT, B_HEADS * TT
                for u in range(NA + 6):
                    if u < NA:
                        h, t = u // TT, u % TT
                        half = slice((h % 2) * HD, (h % 2) * HD + HD)
                        b = sc_open(SC_A + u)
                        mm(b[:, :], qA[half, h // 2, t * P:(t + 1) * P], kA[half, :], start=True, stop=True) \
                            .then_inc(sc_done, 1)
                    if 2 <= u < NA + 2:
                        v = u - 2
                        b = tr_open(TR_A + v)
                        pe.wait_ge(a_scaled, s * (NA + NB) + v + 1)
                        for j in range(4):
                            last = nc.tensor.transpose(b[:, j * P:(j + 1) * P],
                                                       prob[:, (v % 3) * 768 + j * P:(v % 3) * 768 + (j + 1) * P], ident)
                        last.then_inc(tr_done, 1)
                    if u >= 6:
                        h, j = (u - 6) // 4, (u - 6) % 4
                        if j == 0:
                            pv_bank = mm_open(MM_PVA + h)
                            pe.wait_ge(pt_ready, s * (NA + NB * 2) + TT * (h + 1))
                        last = mm(pv_bank[:, :], vA[:, j, :], ptA[h % 2][:, j, :], start=(j == 0), stop=(j == 3))
                        if j == 3:
                            last.then_inc(mm_done, 1)

                pe.wait_ge(b_act, s * 12 + 12)
                pe.wait_ge(b_dve, s * 12 + 12)
                pe.wait_ge(tab_in, 16 * B_HEADS)
                for u in range(NB + 6):
                    if u < NB:
                        h, t = u // TT, u % TT
                        half = slice((h % 2) * HD, (h % 2) * HD + HD)
                        q = [qB[half, 2 * g + h // 2, t * P:(t + 1) * P] for g in range(N_DIL)]
                        b = sc_open(SC_B + 2 * u)
                        mm(b[:, :], q[0], kB[half, h // 2, :], start=True, stop=True).then_inc(sc_done, 1)
                        b = sc_open(SC_B + 2 * u + 1)
                        for g in (1, 2):
                            last = mm(b[:, (g - 1) * P:g * P], q[g], kB[half, 2 * g + h // 2, t * P:(t + 1) * P],
                                      start=True, stop=True)
                        last.then_inc(sc_done, 1)
                    if 2 <= u < NB + 2:
                        v = u - 2
                        pe.wait_ge(a_scaled, s * (NA + NB) + NA + v + 1)
                        for f in range(2):
                            b = tr_open(TR_B + 2 * v + f)
                            for j in range(4 if f == 0 else 2):
                                o = (v % 3) * 768 + (4 * f + j) * P
                                last = nc.tensor.transpose(b[:, j * P:(j + 1) * P], prob[:, o:o + P], ident)
                            last.then_inc(tr_done, 1)
                    if u >= 6:
                        h, j = (u - 6) // 4, (u - 6) % 4
                        pair = (h // 2) * P
                        if j == 0:
                            pv_bank = mm_open(MM_PVB + h)
                            pe.wait_ge(pt_ready, s * (NA + NB * 2) + NA + 2 * TT * (h + 1))
                        mm(pv_bank[:, :], vB[:, j, pair:pair + P], ptB[h % 2][:, j, :], start=(j == 0), stop=False)
                        for g in (1, 2):
                            last = mm(pv_bank[:, j * P:(j + 1) * P], vB[:, j, 256 * g + pair:256 * g + pair + P],
                                      ptB[h % 2][:, 3 + g, j * P:(j + 1) * P], start=False, stop=(g == 2 and j == 3))
                        if j == 3:
                            last.then_inc(mm_done, 1)

                for c in range(C_GATE, C_B):
                    for f in range(2):
                        last = by_feature(c, MM_GATE + 2 * (c - C_GATE) + f, f, KD, xT_v)
                pe.wait_ge(pv_lo, s * 12 + 12)
                for c in range(C_B, C_OUT):
                    for f in range(4):
                        last = by_feature(c, MM_YB + 4 * (c - C_B) + f, f, 2 if c < C_A else 4,
                                          outB_v if c < C_A else outA_v)
                for c in range(C_OUT, N_CHUNK):
                    for t in range(TT):
                        last = by_token(c, MM_OUT + TT * (c - C_OUT) + t, t, xT_v)
                pe.wait_ge(const_in, CONSTS)
                for u in range(TT + 1):
                    if u < TT:
                        t = u
                        pe.wait_ge(x1_ready, s * TT + t + 1)
                        for f in range(2):
                            b = tr_open(TR_X1 + 2 * t + f)
                            for k in range(4):
                                last = nc.tensor.transpose(b[:, k * P:(k + 1) * P],
                                                           xr[:, t, (4 * f + k) * P:(4 * f + k + 1) * P], ident)
                            last.then_inc(tr_done, 1)
                    if u >= 1:
                        t = u - 1
                        b = sc_open(SC_R + t)
                        pe.wait_ge(x1T_ready, s * 2 * TT + 2 * t + 4)
                        for k in range(KD):
                            last = mm(b[:, 0:20], x1T[t % 2][:, k, :], w_route[:, k * 20:(k + 1) * 20],
                                      start=(k == 0), stop=(k == KD - 1))
                        last.then_inc(sc_done, 1)

            pe.wait_ge(member, 1)
            M16 = NT * NE
            mm(bank[2][:, 0:M16], before, rt[:, 0:M16], start=True, stop=False)
            mm(bank[2][:, 0:M16], ones, rt[:, M16:2 * M16], start=False, stop=True)
            mm(bank[3][:, 0:NE], ones, rt[:, 2 * M16:2 * M16 + NE], start=True, stop=True).then_inc(ranked, 1)
            pe.wait_ge(counted, 1)
            passes = pe.value_load(n_pass[0:1, 0:1], min_val=1, max_val=4)

            def turn_rows(b, z, gathers, part):
                pe.wait_ge(rows_in[b], gathers * 32)
                for g in (2 * part, 2 * part + 1):
                    tb = bank[g % 2]
                    pe.wait_ge(xe_lo, z * 4 + g + 1)
                    for q in range(4):
                        k, c = 2 * g + q // 2, q % 2
                        last = nc.tensor.transpose(tb[:, q * P:(q + 1) * P],
                                                   x_rows[b][:, c * D + k * P:c * D + (k + 1) * P], ident)
                    last.then_inc(rows_T, 1)

            turn_rows(0, 0, 1, 0)
            turn_rows(0, 0, 1, 1)

            def step(ps, i, b, width):
                z0 = ps * NE + i * 2
                z = z0 + b
                pe.wait_ge(xe_lo, z * 4 + 4 + 2)
                xv = [t.rearrange("p (k n) -> p k n", k=KD) for t in xe[b]]
                hv = [t.rearrange("p (m n) -> p m n", m=4) for t in hT]

                def turn_acts(c):
                    tb = bank[4 + c]
                    pe.wait_ge(h_done, z * XCH + c + 3)
                    if c == 0:
                        pe.wait_ge(y_act, z * 2 + 1)
                        pe.wait_ge(y_dve, z * 2 + 1)
                    for r in range(width // P):
                        o = (c % 2) * SLOTS + r * P
                        last = nc.tensor.transpose(tb[:, r * P:(r + 1) * P], h_full[:, o:o + P], ident)
                    last.then_inc(h_turned, 1)

                for c in range(XCH):
                    n = b * ECH + c
                    ub = bank[2 + c % 2]
                    pe.wait_ge(h_done, z * XCH + c + 1)
                    pe.wait_ge(e_lo, z0 * ECH + n + RAW_E + 1)
                    w = [t[n % SPLIT_E].rearrange("p (k n) -> p k n", k=KD) for t in (moe_hi, moe_lo)]
                    for r in range(width // P):
                        for k in range(KD):
                            last = mm3(ub[:, r * 2 * P:(r + 1) * 2 * P], [v[:, k, r * P:(r + 1) * P] for v in xv],
                                       [v[:, k] for v in w], k == 0, k == KD - 1)
                    last.then_inc(e_used, 1)
                    if c >= 1:
                        turn_acts(c - 1)
                    if c >= 2:
                        turn_rows(1 - b, z + 1, ps * (NE // 2) + i + (1 if b == 0 else 2), c - 2)
                turn_acts(XCH - 1)
                for c in range(2):
                    n = b * ECH + XCH + c
                    pe.wait_ge(e_lo, z0 * ECH + n + RAW_E + 1)
                    pe.wait_ge(h_lo, z * XCH + 2 * c + 2)
                    w = [t[n % SPLIT_E].rearrange("p (k n) -> p k n", k=2) for t in (moe_hi, moe_lo)]
                    for r in range(width // P):
                        if r == 1 and c == 0:
                            pe.wait_ge(h_lo, z * XCH + 4)
                        for d in range(2):
                            for k in range(2):
                                f = 2 * c + k
                                last = mm3(bank[4 + 2 * r + d][:, :], [v[:, f, r * P:(r + 1) * P] for v in hv],
                                           [v[:, k, d * 512:(d + 1) * 512] for v in w], f == 0, f == 3)
                    last.then_inc(e_used, 1)

            with pe.Fori(0, passes) as ps:
                with pe.Fori(0, NE // 2) as i:
                    for b in range(2):
                        full = pe.value_load(is_full[0:1, bass.ds(ps * NE + i * 2 + b, 1)], min_val=0, max_val=1)
                        with pe.If(full > 0):
                            step(ps, i, b, SLOTS)
                        with pe.Else():
                            step(ps, i, b, P)

        @block.scalar
        def _(act):
            A = nc.scalar.activation
            act.dma_start(rel_sb[0:NBUCKET, :], rel_bias).then_inc(sel_in, 16)
            act.dma_start(sel_sb, bucket_sel).then_inc(sel_in, 16)
            for dst, src in ((cos_q.rearrange("p (t d) -> p t d", t=TT), rope_c),
                             (sin_q.rearrange("p (t d) -> p t d", t=TT), rope_s),
                             (gains[:, 0:HD], q_gain[0].partition_broadcast(P)),
                             (gains[:, HD:2 * HD], k_gain[0].partition_broadcast(P))):
                act.dma_start(dst, src).then_inc(rope_in, 16)
            consts = [(b_route[:, 0:NG], b_rg[0].partition_broadcast(P)),
                      (b_route[:, NG:20], b_re[0].rearrange("g e -> (g e)").partition_broadcast(P)),
                      (before, before_c), (ones, ones_c), (expert_base, expert_base_c), (tie, tie_c),
                      (token_id, token_id_c)]
            w_route_v = w_route.rearrange("p (k n) -> p k n", k=KD)
            with nc.allow_non_contiguous_dma(reason="a few small parameters"):
                consts.append((bgate, b_gate[0].rearrange("(f p) -> p f", p=P)))
                consts.append((w_route_v[:, :, 0:NG], w_rg[0].rearrange("(k p) g -> p k g", p=P)))
                for g in range(NG):
                    consts.append((w_route_v[:, :, NG + EPG * g:NG + EPG * (g + 1)],
                                   w_re[0, g].rearrange("(k p) e -> p k e", p=P)))
                for dst, src in consts:
                    act.dma_start(dst, src).then_inc(const_in, 16)
            assert CONSTS == 16 * len(consts)
            for n in range(0, MM_SETUP, 2):
                g, c0, w = TAB_PIECES[n]
                act.wait_ge(mm_done, n + 1)
                A(tab_sb[:, c0:c0 + w], bank[mm_bank(n)][0:B_HEADS, 0:w], ACT.Copy).then_inc(tab_act, 1)

            with act.Fori(0, SEQS) as s:
                NA, NB = N_KV * GROUP * TT, B_HEADS * TT

                def mm_wait(n):
                    act.wait_ge(mm_done, MM_SETUP + s * MM_N + n + 1)
                    return bank[mm_bank(n)]

                def tr_wait(n):
                    act.wait_ge(tr_done, s * TR_N + n + 1)
                    return bank[n % 2]

                def split_hi(c):
                    shape = chunk_shape(c)
                    act.wait_ge(mm_done, MM_SETUP + s * MM_N + (CHUNK_END[c - 2] if c >= 2 else 0))
                    act.wait_ge(raw_in[c % 2], (s * (N_CHUNK // 2) + c // 2) * 32 + 32)
                    A(view(whi[c % 2], shape), view(raw[c % 2], shape), ACT.Copy).then_inc(w_hi, 1)

                split_hi(0)
                act.wait_ge(mm_done, MM_SETUP + s * MM_N)
                for u in range(2 * TT):
                    t, f = u // 2, u % 2
                    b = tr_wait(TR_X + u)
                    A(xT_v[0][:, 4 * f:4 * f + 4, t * P:(t + 1) * P], b.rearrange("p (k n) -> p k n", k=4), ACT.Copy) \
                        .then_inc(xhi, 1)
                split_hi(1)
                copied = 0
                for c in range(N_QKV):
                    n0, q = MM_QKV[c], QKV[c]
                    if q < 3:
                        if q > 0:
                            act.wait_ge(q_turned, s * 3 + q)
                        for t in range(TT):
                            b = mm_wait(n0 + t)
                            w = 256 if q < 2 else KV_W
                            A(q_raw[:, t, 0:w], b[:, 0:w], ACT.Copy).then_inc(q_copied, 1)
                            if q == 2:
                                A(vA[:, t, :], b[:, KV_W:2 * KV_W], ACT.Copy).then_inc(va_ready, 1)
                        act.wait_ge(q_copied, s * 3 * TT + (q + 1) * TT)
                        w = 256 if q < 2 else KV_W
                        A(q_tmp[:, :, 0:w], q_raw[:, :, 0:w], ACT.Square).then_inc(q_square, 1)
                    elif q <= 8:
                        b = mm_wait(n0)
                        f = 2 * (q - 3)
                        dst = qB[:, f] if f < 6 else kB[:, f - 6]
                        A(dst, b[:, :], ACT.Copy).then_inc(b_act, 1)
                    else:
                        for t in (0, 2):
                            b = mm_wait(n0 + t)
                            A(vB[:, t, (q - 9) * 256:(q - 8) * 256], b[:, 0:256], ACT.Copy) \
                                .then_inc(b_act, 1)
                    if q in (3, 4, 5):
                        m = q - 3
                        act.wait_ge(q_var, s * 3 + m + 1)
                        nh = 16 if m < 2 else 8
                        A(ss[:, m * 16:m * 16 + nh], ss[:, m * 16:m * 16 + nh], ACT.Sqrt).then_inc(q_root, 1)
                    if c + 2 < N_CHUNK:
                        split_hi(c + 2)
                act.wait_ge(tab_out, 16)
                act.wait_ge(slots_zeroed, 16)
                for u in range(TT):
                    b = tr_wait(TR_Q + u)
                    A(qA[:, :, u * P:(u + 1) * P], b.rearrange("p (m n) -> p m n", m=4), ACT.Copy) \
                        .then_inc(qkA_ready, 1)
                for u in range(2):
                    b = tr_wait(TR_K + u)
                    A(kA[:, u * 256:(u + 1) * 256], b[:, 0:256], ACT.Copy) \
                        .then_inc(qkA_ready, 1)

                for u in range(NA + 6):
                    if u < NA:
                        act.wait_ge(a_max, s * (NA + NB) + u + 1)
                        if u >= 3:
                            act.wait_ge(tr_done, s * TR_N + TR_A + u - 2)
                        A(prob[:, (u % 3) * 768:(u % 3) * 768 + 512], bank[sc_bank(SC_A + u)][:, :], ACT.Exp,
                          bias=neg_max[:, u % 4:u % 4 + 1], scale=1.0, accum_out=den[:, u % 4:u % 4 + 1]) \
                            .then_inc(a_exp, 1)
                    if 2 <= u < NA + 2:
                        v = u - 2
                        h, t = v // TT, v % TT
                        b = tr_wait(TR_A + v)
                        if t == 0:
                            if h >= 2:
                                act.wait_ge(mm_done, MM_SETUP + s * MM_N + MM_PVA + h - 1)
                        A(ptA[h % 2][:, :, t * P:(t + 1) * P], b.rearrange("p (j n) -> p j n", j=4), ACT.Copy) \
                            .then_inc(pt_ready, 1)
                    if u >= 9 and (u - 9) % 4 == 0:
                        h = (u - 9) // 4
                        half = slice((h % 2) * HD, (h % 2) * HD + HD)
                        b = mm_wait(MM_PVA + h)
                        A(outA_v[0][half, h // 2, :], b[half, :], ACT.Copy).then_inc(pv_hi, 1)
                for u in range(NB + 6):
                    if u < NB:
                        act.wait_ge(a_max, s * (NA + NB) + NA + u + 1)
                        w = prob[:, (u % 3) * 768:(u % 3) * 768 + 768]
                        A(w, w, ACT.Exp, bias=neg_max[:, u % 4:u % 4 + 1], scale=1.0,
                          accum_out=den[:, u % 4:u % 4 + 1]).then_inc(a_exp, 1)
                    if 2 <= u < NB + 2:
                        v = u - 2
                        h, t = v // TT, v % TT
                        if t == 0:
                            act.wait_ge(mm_done, MM_SETUP + s * MM_N + MM_PVB + max(h - 1, 0))
                        for f in range(2):
                            n = TR_B + 2 * v + f
                            b = tr_wait(n)
                            js = 4 if f == 0 else 2
                            A(ptB[h % 2][:, 4 * f:4 * f + js, t * P:(t + 1) * P], b[:, 0:js * P].rearrange("p (j n) -> p j n", j=js),
                              ACT.Copy).then_inc(pt_ready, 1)
                    if u >= 9 and (u - 9) % 4 == 0:
                        h = (u - 9) // 4
                        half = slice((h % 2) * HD, (h % 2) * HD + HD)
                        b = mm_wait(MM_PVB + h)
                        A(outB_v[0][half, h // 2, :], b[half, :], ACT.Copy).then_inc(pv_hi, 1)
                act.wait_ge(const_in, CONSTS)
                for c in range(C_GATE, N_CHUNK):
                    if c < C_B:
                        for f in range(2):
                            n = 2 * (c - C_GATE) + f
                            b = mm_wait(MM_GATE + n)
                            A(sg[:, n, :], b[:, :], ACT.Sigmoid, bias=bgate[:, n:n + 1]) \
                                .then_inc(gate_ready, 1)
                    if C_A <= c < C_OUT:
                        for f in range(4):
                            n = 4 * (c - C_A) + f
                            act.wait_ge(summed, s * KD + n + 1)
                            A(xT_v[0][:, n, :], gated[:, n, :], ACT.Copy).then_inc(merged_hi, 1)
                    if c + 2 < N_CHUNK:
                        split_hi(c + 2)
                act.wait_ge(ln_var, s + 1)
                A(rstd1, rstd1, ACT.Sqrt).then_inc(ln_root, 1)
                act.wait_ge(ln_scale, s + 1)
                for t in range(TT):
                    A(xr[:, t, :], xr[:, t, :], ACT.Identity, bias=shift1[:, t:t + 1], scale=rstd1[:, t:t + 1]) \
                        .then_inc(ln_normed, 1)
                for t in range(TT):
                    act.wait_ge(x1_ready, s * TT + t + 1)
                    act.dma_start(x1_d[bass.ds(s * SEQ + t * P, P), :], xr[:, t, :]).then_inc(x1_out, 16)
                    for f in range(2):
                        n = TR_X1 + 2 * t + f
                        b = tr_wait(n)
                        if t >= 2:
                            act.wait_ge(sc_done, s * SC_N + SC_R + t - 1)
                        A(x1T[t % 2][:, 4 * f:4 * f + 4, :], b.rearrange("p (k n) -> p k n", k=4), ACT.Copy) \
                            .then_inc(x1T_ready, 1)

            act.wait_ge(r_exp_in, 1)
            A(rt[:, R_G4:R_G4 + NT * NG], rt[:, R_G4:R_G4 + NT * NG], ACT.Exp).then_inc(r_exp, 1)
            act.wait_ge(r_exp_in, 2)
            A(rt[:, R_E2:R_E2 + NT], rt[:, R_E2:R_E2 + NT], ACT.Exp).then_inc(r_exp, 1)
            act.wait_ge(x1_out, 16 * NT + 1)
            for j in range(NT):
                act.dma_start(x1_tile[j], x1_d[j * P:(j + 1) * P, :]).then_inc(x1_back, 16)
            act.wait_ge(counted, 1)
            passes = act.value_load(n_pass[0:1, 0:1], min_val=1, max_val=4)

            def e_split(pair, m):
                act.wait_ge(e_used, pair * 2 * ECH + m + 1)
                act.wait_ge(e_raw[m % RAW_E], (pair * (2 * ECH // RAW_E) + m // RAW_E + 1) * 32)
                A(moe_hi[m % SPLIT_E], moe_raw[m % RAW_E], ACT.Copy).then_inc(e_hi, 1)

            def rows_hi(b, z, part):
                for g in (2 * part, 2 * part + 1):
                    act.wait_ge(rows_T, z * 4 + g + 1 + 8)
                    A(xe[b][0][:, g * 512:(g + 1) * 512], bank[g % 2][:, :], ACT.Copy).then_inc(xe_hi, 1)

            for c in range(SPLIT_E):
                e_split(0, c)
            act.wait_ge(x1_back, 16 * NT)
            for j in range(NT):
                A(x1_tile[j], x1_tile[j], ACT.Copy, scale=ALPHA).then_inc(f_alpha, 1)
            rows_hi(0, 0, 0)
            rows_hi(0, 0, 1)
            with act.Fori(0, passes) as ps:
                with act.Fori(0, NE // 2) as i:
                    pair = ps * (NE // 2) + i
                    for b in range(2):
                        z = pair * 2 + b

                        def acts_hi(c):
                            act.wait_ge(h_turned, z * XCH + c + 3)
                            A(hT[0][:, c * SLOTS:(c + 1) * SLOTS], bank[4 + c][:, 0:SLOTS], ACT.Copy).then_inc(h_hi, 1)

                        for c in range(XCH):
                            act.wait_ge(e_used, SPLIT_E + z * ECH + c + 1)
                            A(silu[:, (c % 2) * SLOTS:(c % 2 + 1) * SLOTS].rearrange("p (r n) -> p r n", r=2),
                              bank[2 + c % 2].rearrange("p (r a n) -> p r a n", r=2, a=2)[:, :, 0], ACT.Silu) \
                                .then_inc(silu_done, 1)
                            if c >= 1:
                                acts_hi(c - 1)
                                if c >= 2:
                                    rows_hi(1 - b, z + 1, c - 2)
                                if c < XCH - 1:
                                    e_split(pair, b * ECH + c - 1 + SPLIT_E)
                        acts_hi(XCH - 1)
                        e_split(pair, b * ECH + XCH - 2 + SPLIT_E)
                        e_split(pair, b * ECH + XCH - 1 + SPLIT_E)
                        e_split(pair, b * ECH + XCH + SPLIT_E)
                        act.wait_ge(e_used, SPLIT_E + z * ECH + ECH)
                        act.wait_ge(y_gone, z + 1)
                        for d in range(2):
                            A(y_sb[b][:, d * 512:(d + 1) * 512], bank[4 + d][:, :], ACT.Copy).then_inc(y_act, 1)
                        e_split(pair, b * ECH + XCH + 1 + SPLIT_E)
            for j in range(NT + 1):
                if j < NT:
                    act.wait_ge(f_var, j + 1)
                    A(fin_scale[:, j:j + 1], fin_scale[:, j:j + 1], ACT.Sqrt).then_inc(f_root, 1)
                if j >= 1:
                    act.wait_ge(f_scale, j)
                    A(x1_tile[j - 1], x1_tile[j - 1], ACT.Identity, bias=fin_shift[:, j - 1:j],
                      scale=fin_scale[:, j - 1:j]).then_inc(f_normed, 1)

        @block.vector
        def _(dve):
            V = nc.vector
            for k, sm in enumerate([w_split] * 2 + [x1T_ready] * 2 + [logit_ready] * 2 + [residual] * 4 + [merged_lo, x1_out, y_gone]):
                V.memset(small[:, k:k + 1], 0.0).then_inc(sm, 1)
            V.memset(rel_sb[NBUCKET:NBUCKET + 1, :], 1.0).then_inc(rel_ready, 1)
            dve.wait_ge(rope_in, 64)
            gq, gk = [gains[:, i * HD:(i + 1) * HD] for i in range(2)]

            def bc(a):
                return a.unsqueeze(1).broadcast_to([P, TT, HD])

            def tab(a):
                return a.rearrange("p (t d) -> p t d", t=TT)

            def half_of(a, u):
                return a.rearrange("p (t a u j) -> p t a u j", t=TT, a=2, u=2)[:, :, :, u]

            def gain_half(g, u):
                return g.rearrange("p (a u j) -> p a u j", a=2, u=2)[:, :, u].unsqueeze(1).broadcast_to([P, TT, 2, 16])

            V.tensor_tensor(tab(cos_k), tab(cos_q), bc(gk), ALU.mult).then_inc(rope_ready, 1)
            for u in range(2):
                ins = V.tensor_tensor(half_of(sin_k, u), half_of(sin_q, u), gain_half(gk, 1 - u), ALU.mult)
            ins.then_inc(rope_ready, 1)
            V.tensor_scalar(gq, gq, SCALE, None, ALU.mult).then_inc(rope_ready, 1)
            dve.wait_ge(rope_ready, 3)
            V.tensor_tensor(tab(cos_q), tab(cos_q), bc(gq), ALU.mult).then_inc(rope_ready, 1)
            for u in range(2):
                ins = V.tensor_tensor(half_of(sin_q, u), half_of(sin_q, u), gain_half(gq, 1 - u), ALU.mult)
            ins.then_inc(rope_ready, 1)
            for n in range(1, MM_SETUP, 2):
                g, c0, w = TAB_PIECES[n]
                dve.wait_ge(mm_done, n + 1)
                V.tensor_copy(tab_sb[:, c0:c0 + w], bank[mm_bank(n)][0:B_HEADS, 0:w]).then_inc(tab_dve, 1)

            chain = Chain(dve, dve_step)
            with dve.Fori(0, SEQS) as s:
                NA, NB = N_KV * GROUP * TT, B_HEADS * TT
                chain.n, chain.base = 0, s * DVE_CHAIN_SEQ

                def mm_wait(n):
                    dve.wait_ge(mm_done, MM_SETUP + s * MM_N + n + 1)
                    return bank[mm_bank(n)]

                def split_lo(c):
                    shape = chunk_shape(c)
                    dve.wait_ge(w_hi, s * N_CHUNK + c + 1)
                    V.tensor_tensor(view(wlo[c % 2], shape), view(raw[c % 2], shape),
                                    view(whi[c % 2], shape).bitcast(F32), ALU.subtract).then_inc(w_split, 1)

                split_lo(0)
                for u in range(2 * TT):
                    t, f = u // 2, u % 2
                    dve.wait_ge(xhi, s * 2 * TT + u + 1)
                    V.tensor_tensor(xT_v[1][:, 4 * f:4 * f + 4, t * P:(t + 1) * P],
                                    bank[u % 2][:, :].rearrange("p (k n) -> p k n", k=4),
                                    xT_v[0][:, 4 * f:4 * f + 4, t * P:(t + 1) * P].bitcast(F32), ALU.subtract) \
                        .then_inc(xlo, 1)
                split_lo(1)
                for c in range(N_QKV):
                    n0, q = MM_QKV[c], QKV[c]
                    if q < 3:
                        w, nh = (256, 16) if q < 2 else (KV_W, 8)
                        sq = q_tmp[:, :, 0:w].rearrange("p t (h d) -> p t h d", d=HD)
                        r = ss[:, q * 16:q * 16 + nh]
                        dve.wait_ge(q_square, s * 3 + q + 1)
                        chain(V.tensor_reduce(r, sq, X, ALU.add))
                        V.tensor_scalar(r, r, 1.0 / HD, RMS_EPS, ALU.mult, ALU.add).then_inc(q_var, 1)
                    elif q <= 8:
                        b = mm_wait(n0 + 1)
                        f = 2 * (q - 3) + 1
                        dst = qB[:, f] if f < 6 else kB[:, f - 6]
                        V.tensor_copy(dst, b[:, :]).then_inc(b_dve, 1)
                    else:
                        for t in (1, 3):
                            b = mm_wait(n0 + t)
                            V.tensor_copy(vB[:, t, (q - 9) * 256:(q - 8) * 256], b[:, 0:256]) \
                                .then_inc(b_dve, 1)
                    if q in (3, 4, 5):
                        m = q - 3
                        w, nh = (256, 4) if m < 2 else (KV_W, 2)
                        r = ss[:, m * 16:m * 16 + TT * nh]
                        dve.wait_ge(q_root, s * 3 + m + 1)
                        chain(V.reciprocal(r, r))
                        v = q_raw[:, :, 0:w].rearrange("p t (h d) -> p t h d", d=HD)
                        V.tensor_tensor(v, v, r.rearrange("p (t h) -> p t h", t=TT).unsqueeze(3)
                                        .broadcast_to([P, TT, nh, HD]), ALU.mult).then_inc(q_normed, 1)
                    if c + 2 < N_CHUNK:
                        split_lo(c + 2)

                def normalise(v, width, base):
                    dve.wait_ge(a_exp, s * (NA + NB) + base + v + 1)
                    chain(V.reciprocal(rden[:, v % 4:v % 4 + 1], den[:, v % 4:v % 4 + 1]))
                    w = prob[:, (v % 3) * 768:(v % 3) * 768 + width]
                    V.tensor_scalar(w, w, rden[:, v % 4:v % 4 + 1], None, ALU.mult).then_inc(a_scaled, 1)

                for u in range(NA + 6):
                    if u < NA:
                        dve.wait_ge(sc_done, s * SC_N + SC_A + u + 1)
                        V.tensor_reduce(neg_max[:, u % 4:u % 4 + 1], bank[sc_bank(SC_A + u)][:, :], X, ALU.max, negate=True) \
                            .then_inc(a_max, 1)
                    if 1 <= u <= NA:
                        normalise(u - 1, 512, 0)
                    if u >= 9 and (u - 9) % 4 == 0:
                        h = (u - 9) // 4
                        half = slice((h % 2) * HD, (h % 2) * HD + HD)
                        dve.wait_ge(pv_hi, s * 12 + h + 1)
                        V.tensor_tensor(outA_v[1][half, h // 2, :], bank[mm_bank(MM_PVA + h)][half, :],
                                        outA_v[0][half, h // 2, :].bitcast(F32), ALU.subtract) \
                            .then_inc(pv_lo, 1)
                for u in range(NB + 6):
                    if u < NB:
                        h, t = u // TT, u % TT
                        w = prob[:, (u % 3) * 768:(u % 3) * 768 + 768]
                        dve.wait_ge(tr_done, s * TR_N + (TR_B + 2 * (u - 2) if u >= 3 else TR_B))
                        dve.wait_ge(sc_done, s * SC_N + SC_B + 2 * u + 1)
                        V.scalar_tensor_tensor(w[:, 0:512], bank[6][:, :], SCALE,
                                               tabs[:, h, 3 - t:7 - t].rearrange("p b n -> p (b n)"),
                                               ALU.mult, ALU.add).then_inc(b_logit, 1)
                        dve.wait_ge(sc_done, s * SC_N + SC_B + 2 * u + 2)
                        V.scalar_tensor_tensor(w[:, 512:768], bank[7][:, 0:256], SCALE,
                                                     tabs[:, h, 7:9].rearrange("p b n -> p (b n)"),
                                                     ALU.mult, ALU.add).then_inc(b_logit, 1)
                        dve.wait_ge(b_logit, s * 2 * NB + 2 * u + 2)
                        V.tensor_reduce(neg_max[:, u % 4:u % 4 + 1], w, X, ALU.max, negate=True).then_inc(a_max, 1)
                    if 1 <= u <= NB:
                        normalise(u - 1, 768, NA)
                    if u >= 9 and (u - 9) % 4 == 0:
                        h = (u - 9) // 4
                        half = slice((h % 2) * HD, (h % 2) * HD + HD)
                        dve.wait_ge(pv_hi, s * 12 + 8 + h + 1)
                        V.tensor_tensor(outB_v[1][half, h // 2, :], bank[mm_bank(MM_PVB + h)][half, :],
                                        outB_v[0][half, h // 2, :].bitcast(F32), ALU.subtract) \
                            .then_inc(pv_lo, 1)

                def merge_lo(n):
                    dve.wait_ge(merged_hi, s * KD + n + 1)
                    V.tensor_tensor(xT_v[1][:, n, :], gated[:, n, :], xT_v[0][:, n, :].bitcast(F32),
                                    ALU.subtract).then_inc(merged_lo, 1)

                for c in range(C_GATE, N_CHUNK):
                    if C_B <= c < C_A:
                        for f in range(4):
                            n = 4 * (c - C_B) + f
                            b = mm_wait(MM_YB + n)
                            dve.wait_ge(gate_ready, s * 16 + KD + n + 1)
                            V.tensor_tensor(gated[:, n, :], b[:, :], sg[:, KD + n, :], ALU.mult) \
                                .then_inc(yb_used, 1)
                    if C_A <= c < C_OUT:
                        for f in range(4):
                            n = 4 * (c - C_A) + f
                            b = mm_wait(MM_YA + n)
                            dve.wait_ge(gate_ready, s * 16 + n + 1)
                            V.tensor_tensor(sg[:, n, :], b[:, :], sg[:, n, :], ALU.mult).then_inc(ya_used, 1)
                            if n >= 2:
                                merge_lo(n - 2)
                            if n == KD - 1:
                                merge_lo(n - 1)
                                merge_lo(n)
                    if c >= C_OUT:
                        if c == C_OUT:
                            dve.wait_ge(xr_in, s * 16 + 16)
                        col = slice((c - C_OUT) * 256, (c - C_OUT + 1) * 256)
                        for t in range(TT):
                            n = MM_OUT + TT * (c - C_OUT) + t
                            b = mm_wait(n)
                            V.scalar_tensor_tensor(xr[:, t, col], xr[:, t, col], ALPHA, b[:, 0:256], ALU.mult, ALU.add) \
                                .then_inc(residual, 1)
                            dve.wait_ge(residual, s * TT * N_OUT + n - MM_OUT + 1 + 4)
                            o = (t * N_OUT + c - C_OUT) * 6
                            ins = V.bn_stats(stats[:, o:o + 6], xr[:, t, col])
                    if c + 2 < N_CHUNK:
                        split_lo(c + 2)
                chain(ins)
                V.memset(small[:, 62:63], 0.0)
                for t in range(TT):
                    ins = V.bn_aggr(mv[:, 2 * t:2 * t + 2], stats[:, t * N_OUT * 6:(t + 1) * N_OUT * 6])
                chain(ins)
                mean, var = [mv.rearrange("p (t a) -> p t a", a=2)[:, :, a] for a in range(2)]
                V.tensor_scalar(rstd1, var, LN_EPS, None, ALU.add).then_inc(ln_var, 1)
                dve.wait_ge(ln_root, s + 1)
                chain(V.reciprocal(rstd1, rstd1))
                V.scalar_tensor_tensor(shift1, mean, -1.0, rstd1, ALU.mult, ALU.mult).then_inc(ln_scale, 1)
                dve.wait_ge(lnp_in, s * 32 + 32)
                for t in range(TT):
                    dve.wait_ge(ln_normed, s * TT + t + 1)
                    V.tensor_tensor(xr[:, t, :], xr[:, t, :], lnp[:, 0], ALU.mult).then_inc(ln_gained, 1)
                    if t == 0:
                        dve.wait_ge(ln_gained, s * TT + 1)
                        V.tensor_tensor(xr[:, t, :], xr[:, t, :], lnp[:, 1], ALU.add).then_inc(x1_ready, 1)
                dve.wait_ge(const_in, CONSTS)
                for t in range(TT):
                    dve.wait_ge(sc_done, s * SC_N + SC_R + t + 1)
                    V.tensor_tensor(logits[:, bass.ds((s * TT + t) * 20, 20)], bank[sc_bank(SC_R + t)][:, 0:20],
                                    b_route, ALU.add).then_inc(logit_ready, 1)
                if chain.n != DVE_CHAIN_SEQ:
                    raise ValueError(f"DVE_CHAIN_SEQ is {chain.n}")

            dve.wait_ge(logit_ready, NT + 2)
            used = 16
            for sm, k in ((e_used, SPLIT_E), (e_lo, RAW_E), (rows_T, 8), (xe_lo, 2), (h_done, 2), (h_turned, 2), (y_act, 1), (y_dve, 1)):
                for _i in range(k):
                    V.memset(small[:, used:used + 1], 0.0).then_inc(sm, 1)
                    used += 1
            chain.n, chain.base = 0, SEQS * DVE_CHAIN_SEQ
            M16 = NT * NE
            lg = logits.rearrange("p (t n) -> p t n", n=20)
            area = [2 * M16 + NE]

            def r(n):
                a = rt[:, area[0]:area[0] + n]
                area[0] += n
                return a

            def bc4(a):
                return a.unsqueeze(2).broadcast_to([P, NT, 4])

            def tt(dst, a, b, op):
                chain(V.tensor_tensor(dst, a, b, op))

            def t4(a):
                return a.rearrange("p (t n) -> p t n", n=4)

            tie_b = tie.unsqueeze(1).broadcast_to([P, NT, 4])

            def first_max(dst, src, mx, tmp, tm):
                chain(V.tensor_reduce(mx, src, X, ALU.max))
                tt(t4(tmp), src, bc4(mx), ALU.is_equal)
                tt(t4(tmp), t4(tmp), tie_b, ALU.mult)
                chain(V.tensor_reduce(tm, t4(tmp), X, ALU.max))
                tt(dst, t4(tmp), bc4(tm), ALU.is_equal)

            g_hot, tmp, tm, gmax = r(NT * 4), r(NT * 4), r(NT), r(NT)
            first_max(t4(g_hot), lg[:, :, 0:4], gmax, tmp, tm)
            g4, e2 = rt[:, R_G4:R_G4 + NT * 4], rt[:, R_E2:R_E2 + NT]
            V.tensor_tensor(t4(g4), lg[:, :, 0:4], bc4(gmax), ALU.subtract).then_inc(r_exp_in, 1)
            prod, sel = r(M16), r(NT * 4)
            pv = prod.rearrange("p (t g e) -> p t g e", g=4, e=4)
            tt(pv, lg[:, :, 4:20].rearrange("p t (g e) -> p t g e", g=4),
               t4(g_hot).unsqueeze(3).broadcast_to([P, NT, 4, 4]), ALU.mult)
            chain(V.tensor_reduce(t4(sel), pv.rearrange("p t g e -> p t e g"), X, ALU.add))
            hot1, hot2, m1, m2 = r(NT * 4), r(NT * 4), r(NT), r(NT)
            first_max(t4(hot1), t4(sel), m1, tmp, tm)
            chain(V.scalar_tensor_tensor(sel, hot1, NEG, sel, ALU.mult, ALU.add))
            first_max(t4(hot2), t4(sel), m2, tmp, tm)
            V.tensor_tensor(e2, m2, m1, ALU.subtract).then_inc(r_exp_in, 1)
            one1, one2 = r(M16), r(M16)
            for one, hot in ((one1, hot1), (one2, hot2)):
                tt(one.rearrange("p (t g e) -> p t g e", g=4, e=4), t4(g_hot).unsqueeze(3).broadcast_to([P, NT, 4, 4]),
                   t4(hot).unsqueeze(2).broadcast_to([P, NT, 4, 4]), ALU.mult)
            tt(rt[:, 0:M16], one1, one2, ALU.add)
            chain(V.memset(rt[:, M16:M16 + NE], 0.0))
            for j in range(1, NT + 1):
                o = M16 + j * NE
                ins = V.tensor_tensor(rt[:, o:o + NE], rt[:, o - NE:o], rt[:, (j - 1) * NE:j * NE], ALU.add)
                if j < NT:
                    chain(ins)
            ins.then_inc(member, 1)
            dve.wait_ge(ranked, 1)
            where = r(M16)
            wv = bank[2][:, 0:M16]
            chain(V.tensor_scalar(where, wv, float(SLOTS), float((NE - 1) * SLOTS), ALU.is_ge, ALU.mult))
            for k in (2, 3):
                chain(V.tensor_scalar(prod, wv, float(SLOTS * k), float((NE - 1) * SLOTS), ALU.is_ge, ALU.mult))
                tt(where, where, prod, ALU.add)
            tt(where, where, wv, ALU.add)
            eb = expert_base.unsqueeze(1).broadcast_to([P, NT, NE])
            tt(where.rearrange("p (t e) -> p t e", e=NE), where.rearrange("p (t e) -> p t e", e=NE), eb, ALU.add)
            for k, one in enumerate((one1, one2)):
                tt(prod, one, where, ALU.mult)
                chain(V.tensor_reduce(tmp[:, k * NT:(k + 1) * NT], prod.rearrange("p (t e) -> p t e", e=NE), X, ALU.add))
            V.tensor_copy(pos_i, tmp[:, 0:2 * NT]).then_inc(placed, 1)
            over3, most = r(4), r(1)
            chain(V.tensor_reduce(most, bank[3][:, 0:NE], X, ALU.max))
            for k in range(3):
                V.tensor_scalar(over3[:, k:k + 1], most, float(SLOTS * (k + 1)), None, ALU.is_gt)
            chain(V.memset(over3[:, 3:4], 1.0))
            chain(V.tensor_reduce(most, over3, X, ALU.add))
            full_f = r(MAXTOK // SLOTS * NE)
            for k in range(MAXTOK // SLOTS):
                ins = V.tensor_scalar(full_f[:, k * NE:(k + 1) * NE], bank[3][:, 0:NE], float(SLOTS * k + P), None, ALU.is_gt)
            chain(ins)
            chain(V.tensor_copy(is_full, full_f))
            V.tensor_copy(n_pass[:, 0:1], most).then_inc(counted, 1)
            dve.wait_ge(r_exp, 2)
            gp = r(NT)
            chain(V.tensor_reduce(gp, t4(g4), X, ALU.add))
            chain(V.reciprocal(gp, gp))
            chain(V.tensor_scalar(m1, e2, 1.0, None, ALU.add))
            chain(V.reciprocal(m1, m1))
            tt(gate[:, 0:NT], m1, gp, ALU.mult)
            tt(gate[:, NT:2 * NT], gate[:, 0:NT], e2, ALU.mult)

            dve.wait_ge(counted, 1)
            passes = dve.value_load(n_pass[0:1, 0:1], min_val=1, max_val=4)

            def e_split(pair, m):
                dve.wait_ge(e_hi, pair * 2 * ECH + m + 1)
                V.tensor_tensor(moe_lo[m % SPLIT_E], moe_raw[m % RAW_E], moe_hi[m % SPLIT_E].bitcast(F32),
                                ALU.subtract).then_inc(e_lo, 1)

            def rows_lo(b, z, part):
                for g in (2 * part, 2 * part + 1):
                    dve.wait_ge(xe_hi, z * 4 + g + 1)
                    V.tensor_tensor(xe[b][1][:, g * 512:(g + 1) * 512], bank[g % 2][:, :],
                                    xe[b][0][:, g * 512:(g + 1) * 512].bitcast(F32), ALU.subtract).then_inc(xe_lo, 1)

            for c in range(SPLIT_E):
                e_split(0, c)
            rows_lo(0, 0, 0)
            rows_lo(0, 0, 1)
            with dve.Fori(0, passes) as ps:
                with dve.Fori(0, NE // 2) as i:
                    pair = ps * (NE // 2) + i
                    for b in range(2):
                        z = pair * 2 + b

                        def acts_lo(c):
                            dve.wait_ge(h_hi, z * XCH + c + 1)
                            V.tensor_tensor(hT[1][:, c * SLOTS:(c + 1) * SLOTS], bank[4 + c][:, 0:SLOTS],
                                            hT[0][:, c * SLOTS:(c + 1) * SLOTS].bitcast(F32), ALU.subtract).then_inc(h_lo, 1)

                        for c in range(XCH):
                            dve.wait_ge(h_turned, z * XCH + c + 1)
                            dve.wait_ge(silu_done, z * XCH + c + 1)
                            half = slice((c % 2) * SLOTS, (c % 2 + 1) * SLOTS)
                            V.tensor_tensor(h_full[:, half].rearrange("p (r n) -> p r n", r=2),
                                            silu[:, half].rearrange("p (r n) -> p r n", r=2),
                                            bank[2 + c % 2].rearrange("p (r a n) -> p r a n", r=2, a=2)[:, :, 1],
                                            ALU.mult).then_inc(h_done, 1)
                            if c >= 1:
                                acts_lo(c - 1)
                                if c >= 2:
                                    rows_lo(1 - b, z + 1, c - 2)
                                if c < XCH - 1:
                                    e_split(pair, b * ECH + c - 1 + SPLIT_E)
                        acts_lo(XCH - 1)
                        e_split(pair, b * ECH + XCH - 2 + SPLIT_E)
                        e_split(pair, b * ECH + XCH - 1 + SPLIT_E)
                        e_split(pair, b * ECH + XCH + SPLIT_E)
                        dve.wait_ge(e_used, SPLIT_E + z * ECH + ECH)
                        dve.wait_ge(y_gone, z + 1)
                        for d in range(2):
                            ins = V.tensor_copy(y_sb[b][:, D + d * 512:D + (d + 1) * 512], bank[6 + d][:, :])
                            ins.then_inc(y_dve, 1)
                        e_split(pair, b * ECH + XCH + 1 + SPLIT_E)

            V.memset(small[:, 61:62], 0.0).then_inc(experts_dve, 1)

            chain.n, chain.base = 0, 0
            chain.sem = f_step
            for j in range(NT + 1):
                if j < NT:
                    cx, st = x1_tile[j], fin_stats[:, 16 * j:16 * j + 12]
                    dve.wait_ge(f_alpha, j + 1)
                    dve.wait_ge(comb_in[j], 32)
                    for k in range(2):
                        chain(V.scalar_tensor_tensor(cx, y_tile[j][k], gate[:, k * NT + j:k * NT + j + 1], cx, ALU.mult, ALU.add))
                    for f in range(2):
                        ins = V.bn_stats(st[:, 6 * f:6 * f + 6], cx[:, f * 512:(f + 1) * 512])
                    chain(ins)
                    chain(V.bn_aggr(fin_mv[:, 2 * j:2 * j + 2], st))
                    V.tensor_scalar(fin_scale[:, j:j + 1], fin_mv[:, 2 * j + 1:2 * j + 2], LN_EPS, None, ALU.add).then_inc(f_var, 1)
                if j >= 1:
                    i = j - 1
                    dve.wait_ge(f_root, j)
                    chain(V.reciprocal(fin_scale[:, i:j], fin_scale[:, i:j]))
                    V.scalar_tensor_tensor(fin_shift[:, i:j], fin_mv[:, 2 * i:2 * i + 1], -1.0, fin_scale[:, i:j],
                                           ALU.mult, ALU.mult).then_inc(f_scale, 1)
            dve.wait_ge(ln2_in, 32)
            for j in range(POOL_TILES, NT):
                dve.wait_ge(f_normed, j + 1)
                chain(V.tensor_tensor(x1_tile[j], x1_tile[j], ln2p[:, 0:D], ALU.mult))
                V.tensor_tensor(x1_tile[j], x1_tile[j], ln2p[:, D:2 * D], ALU.add).then_inc(f_last, 1)


R_G4 = 2 * NT * NE + NE + 1200
R_E2 = R_G4 + NT * NG


def rope_tables():
    t = np.arange(SEQ)
    inv = 10000.0 ** (-np.arange(0, 32, 2, dtype=np.float32) / np.float32(32))
    ang = np.stack([(t // 64)[:, None] * inv[None], (t % 64)[:, None] * inv[None]], 1).astype(np.float32)
    c, s = np.cos(ang), np.sin(ang)
    cos = np.stack([c, c], 2).reshape(SEQ, HD)
    sin = np.stack([-s, s], 2).reshape(SEQ, HD)
    return [np.ascontiguousarray(a.reshape(P, TT, HD), dtype=np.float32) for a in (cos, sin)]


def bucket_rows():
    sel = np.zeros((NBUCKET + 1, 9, 256), np.float32)
    for blk in range(9):
        for u in range(255):
            d = u - (P - 1)
            if blk < 7:
                rel = 4 * d + blk - 3
                ok = abs(rel) <= 64
            elif blk == 7:
                rel, ok = 4 * d, abs(d) <= 64
            else:
                rel, ok = 4 * d, d % 4 == 0
            if not ok:
                sel[NBUCKET, blk, u] = NEG
                continue
            n = abs(rel)
            big = 8 + int(np.log(np.float32(max(n, 1)) / np.float32(8)) / np.float32(math.log(128)) * np.float32(8))
            sel[(16 if rel > 0 else 0) + (n if n < 8 else min(big, 15)), blk, u] = 1.0
    return sel.reshape(NBUCKET + 1, TAB)


def token_rows():
    tok = np.arange(P)[:, None, None] + P * np.arange(NT)[None, None, :]
    tok = np.broadcast_to(tok, (P, 2, NT))
    return np.stack([tok, tok + MAXTOK * np.arange(2)[None, :, None]], -1).reshape(P, 4 * NT).astype(np.int32)


_INS = ['w_in', 'b_gate', 'q_gain', 'k_gain', 'rel_bias', 'w_branch_a', 'w_branch_b', 'w_out', 'ln1_g', 'ln1_b',
        'w_route_group', 'b_route_group', 'w_route_expert', 'b_route_expert', 'w_expert_in', 'w_expert_out', 'ln2_g', 'ln2_b']


def kernel(**inputs):
    import numpy as _np
    import concourse.bacc as _bacc
    from concourse import mybir as _mybir
    from concourse.bass_utils import run_bass_kernel_spmd as _run

    nc = _bacc.Bacc("TRN2", target_bir_lowering=False, num_devices=1)
    arrays = {"x": _np.concatenate([_np.asarray(inputs["x_prompt"]), _np.asarray(inputs["x_sample"])], 0)}
    for n in _INS:
        arrays[n] = _np.ascontiguousarray(inputs[n])
    rc, rs = rope_tables()
    arrays.update(rope_c=rc, rope_s=rs, bucket_sel=bucket_rows(), ident_c=_np.eye(P, dtype=_np.float32),
                  before_c=_np.triu(_np.ones((P, P), _np.float32), 1), ones_c=_np.ones((P, P), _np.float32),
                  expert_base_c=_np.tile(_np.arange(NE, dtype=_np.float32) * SLOTS, (P, 1)),
                  token_id_c=token_rows(),
                  tie_c=_np.tile(_np.array([4, 3, 2, 1], _np.float32), (P, 1)))
    args = [nc.dram_tensor(f"in_{n}", a.shape, _mybir.dt.from_np(a.dtype), kind="ExternalInput").ap()
            for n, a in arrays.items()]
    args.append(nc.dram_tensor("out_dram", [SEQS, SEQ, D], _mybir.dt.float32, kind="ExternalOutput").ap())
    encoder_kernel(nc, *args)
    r = _run(nc, [{f"in_{n}": a for n, a in arrays.items()}], core_ids=[0])
    y = r.results[0]["out_dram"]
    return y[0:1], y[1:2]
```
